# Optimizing a Trainium2 kernel written in Bass

```python
import math
import jax, jax.numpy as jnp
from jax import lax
import numpy as np
import jax
import jax.numpy as jnp

D_MODEL = 2048
BATCH = 1
SEQ = 256
DEPTH = 2

CHUNK = 64
Q_BLOCK = 128
NORM_EPS = 1e-6

A_HEADS = 8
A_HEAD_DIM = 128
IDX_HEADS = 16
IDX_DIM = 64
TOPK_MAX = 256
POOL_WINDOWS = (2, 4, 8, 16)
POOL_GROUP = 256
POOL_WIDTH = POOL_GROUP * len(POOL_WINDOWS)
C_HEADS = 8
Q_LORA = 512
KV_LORA = 256
QK_NOPE = 128
QK_ROPE = 64
V_HEAD = 128
ROPE_THETA = 10000.0
LRU_WIDTH = 1024
LRU_BLOCKS = 8
LRU_CONV = 4
LRU_C = 8.0
D_FF = 4096
FFN_CONV = 3

A_WIDTH = A_HEADS * A_HEAD_DIM
AB_IN = 3 * A_WIDTH + IDX_HEADS * IDX_DIM + IDX_DIM + IDX_HEADS + POOL_WIDTH
AB_OUT = A_WIDTH + POOL_WIDTH
CD_IN = Q_LORA + KV_LORA + QK_ROPE + 2 * LRU_WIDTH
CD_OUT = C_HEADS * V_HEAD + LRU_WIDTH
N_EVEN = (DEPTH + 1) // 2
N_ODD = DEPTH // 2


def rms_norm(x, g):
    xf = x.astype(jnp.float32)
    y = xf * lax.rsqrt(jnp.mean(xf * xf, axis=-1, keepdims=True) + NORM_EPS)
    return (y * g.astype(jnp.float32)).astype(x.dtype)

def causal_dwconv(x, w, b):
    K = w.shape[0]
    T = x.shape[1]
    xp = jnp.pad(x, ((0, 0), (K - 1, 0), (0, 0)))
    y = xp[:, 0:T] * w[0]
    for k in range(1, K):
        y = y + xp[:, k:k + T] * w[k]
    return y + b

def chunk_limit(q_pos):
    return (q_pos // CHUNK + 1) * CHUNK

def rope(x, pos):
    half = x.shape[-1] // 2
    freq = ROPE_THETA ** (-jnp.arange(half, dtype=jnp.float32) / half)
    ang = pos.astype(jnp.float32)[:, :, None, None] * freq
    cos, sin = jnp.cos(ang), jnp.sin(ang)
    xf = x.astype(jnp.float32)
    x1, x2 = xf[..., :half], xf[..., half:]
    return jnp.concatenate([x1 * cos - x2 * sin, x2 * cos + x1 * sin], axis=-1).astype(x.dtype)

def dsa_attention(q, k, v, q_idx, k_idx, w_idx):
    Bsz, T = q.shape[:2]
    k_top = min(TOPK_MAX, T // 4)
    n_blocks = T // Q_BLOCK
    key_pos = jnp.arange(T)
    idx_scale = (IDX_DIM ** -0.5) * (IDX_HEADS ** -0.5)
    att_scale = A_HEAD_DIM ** -0.5

    def block(i):
        start = i * Q_BLOCK
        qb = lax.dynamic_slice_in_dim(q, start, Q_BLOCK, 1)
        qib = lax.dynamic_slice_in_dim(q_idx, start, Q_BLOCK, 1)
        wb = lax.dynamic_slice_in_dim(w_idx, start, Q_BLOCK, 1)
        limit = chunk_limit(start + jnp.arange(Q_BLOCK))
        admissible = key_pos[None, :] < limit[:, None]
        logits = jnp.einsum('bqhd,bsd->bqhs', qib, k_idx, preferred_element_type=jnp.float32)
        score = jnp.einsum('bqhs,bqh->bqs', jax.nn.relu(logits), wb.astype(jnp.float32)) * idx_scale
        score = jnp.where(admissible[None], score, -jnp.inf)
        _, sel = lax.top_k(score, k_top)
        sel_ok = sel < limit[None, :, None]
        k_sel = jax.vmap(lambda kb, ib: kb[ib])(k, sel)
        v_sel = jax.vmap(lambda vb, ib: vb[ib])(v, sel)
        s = jnp.einsum('bqhd,bqkhd->bhqk', qb, k_sel, preferred_element_type=jnp.float32) * att_scale
        s = jnp.where(sel_ok[:, None], s, -jnp.inf)
        p = jax.nn.softmax(s, axis=-1)
        return jnp.einsum('bhqk,bqkhd->bqhd', p.astype(v.dtype), v_sel)

    out = lax.map(block, jnp.arange(n_blocks))
    return jnp.moveaxis(out, 0, 1).reshape(Bsz, T, A_WIDTH)

def multiscale_pool(u, w, b, scale):
    Bsz, T, _ = u.shape
    G = len(POOL_WINDOWS)
    uf = u.reshape(Bsz, T, G, POOL_GROUP).astype(jnp.float32)
    csum = jnp.cumsum(uf, axis=1)
    t = jnp.arange(T)
    outs = []
    for g, win in enumerate(POOL_WINDOWS):
        c = csum[:, :, g]
        c_prev = jnp.pad(c, ((0, 0), (win, 0), (0, 0)))[:, :T]
        count = jnp.minimum(t + 1, win).astype(jnp.float32)[None, :, None]
        outs.append((c - c_prev) / count - uf[:, :, g])
    pooled = jnp.stack(outs, axis=2).astype(u.dtype)
    mixed = jnp.einsum('btgc,gcd->btgd', pooled, w) + b
    return mixed.reshape(Bsz, T, POOL_WIDTH) * scale

def mla_attention(c_q, c_kv, k_rope_in, positions, q_norm_g, w_q_up, kv_norm_g, w_kv_up):
    Bsz, T = c_q.shape[:2]
    q = (rms_norm(c_q, q_norm_g) @ w_q_up).reshape(Bsz, T, C_HEADS, QK_NOPE + QK_ROPE)
    kv = (rms_norm(c_kv, kv_norm_g) @ w_kv_up).reshape(Bsz, T, C_HEADS, QK_NOPE + V_HEAD)
    q_nope = q[..., :QK_NOPE]
    q_rope = rope(q[..., QK_NOPE:], positions)
    k_nope = kv[..., :QK_NOPE]
    v = kv[..., QK_NOPE:]
    k_rope = rope(k_rope_in[:, :, None, :], positions)[:, :, 0]
    scale = (QK_NOPE + QK_ROPE) ** -0.5
    key_pos = jnp.arange(T)
    n_blocks = T // Q_BLOCK

    def block(i):
        start = i * Q_BLOCK
        qn = lax.dynamic_slice_in_dim(q_nope, start, Q_BLOCK, 1)
        qr = lax.dynamic_slice_in_dim(q_rope, start, Q_BLOCK, 1)
        limit = chunk_limit(start + jnp.arange(Q_BLOCK))
        admissible = key_pos[None, :] < limit[:, None]
        s = (jnp.einsum('bqhd,bshd->bhqs', qn, k_nope, preferred_element_type=jnp.float32)
             + jnp.einsum('bqhr,bsr->bhqs', qr, k_rope, preferred_element_type=jnp.float32)) * scale
        s = jnp.where(admissible[None, None], s, -jnp.inf)
        p = jax.nn.softmax(s, axis=-1)
        return jnp.einsum('bhqs,bshd->bqhd', p.astype(v.dtype), v)

    out = lax.map(block, jnp.arange(n_blocks))
    return jnp.moveaxis(out, 0, 1).reshape(Bsz, T, C_HEADS * V_HEAD)

def rg_lru_branch(x_in, y_in, conv_w, conv_b, wa, ba, wx, bx, lam):
    Bsz, T, _ = x_in.shape
    xc = causal_dwconv(x_in, conv_w, conv_b)
    xb = xc.reshape(Bsz, T, LRU_BLOCKS, LRU_WIDTH // LRU_BLOCKS)
    gate_r = jax.nn.sigmoid(jnp.einsum('btnc,ncd->btnd', xb, wa).reshape(Bsz, T, LRU_WIDTH) + ba)
    gate_i = jax.nn.sigmoid(jnp.einsum('btnc,ncd->btnd', xb, wx).reshape(Bsz, T, LRU_WIDTH) + bx)
    log_a = (-LRU_C * gate_r.astype(jnp.float32)) * jax.nn.softplus(-lam.astype(jnp.float32))
    a = jnp.exp(log_a)
    mult = jnp.sqrt(-jnp.expm1(2.0 * log_a))
    bterm = mult * (gate_i * xc).astype(jnp.float32)

    def combine(lhs, rhs):
        a_l, b_l = lhs
        a_r, b_r = rhs
        return a_l * a_r, a_r * b_l + b_r

    _, h = lax.associative_scan(combine, (a, bterm), axis=1)
    return h.astype(x_in.dtype) * jax.nn.gelu(y_in, approximate=True)

def mixer_ab(h, w_in, pool_w, pool_b, pool_scale, w_out):
    Bsz, T, _ = h.shape
    z = h @ w_in
    sizes = [A_WIDTH, A_WIDTH, A_WIDTH, IDX_HEADS * IDX_DIM, IDX_DIM, IDX_HEADS]
    cuts = [int(c) for c in np.cumsum(sizes)]
    q, k, v, qi, ki, wi, u = jnp.split(z, cuts, axis=-1)
    heads = (Bsz, T, A_HEADS, A_HEAD_DIM)
    a_out = dsa_attention(q.reshape(heads), k.reshape(heads), v.reshape(heads),
                          qi.reshape(Bsz, T, IDX_HEADS, IDX_DIM), ki, wi)
    b_out = multiscale_pool(u, pool_w, pool_b, pool_scale)
    return jnp.concatenate([a_out, b_out], axis=-1) @ w_out

def mixer_cd(h, positions, w_in, q_norm_g, w_q_up, kv_norm_g, w_kv_up,
             conv_w, conv_b, wa, ba, wx, bx, lam, w_out):
    z = h @ w_in
    sizes = [Q_LORA, KV_LORA, QK_ROPE, LRU_WIDTH]
    cuts = [int(c) for c in np.cumsum(sizes)]
    c_q, c_kv, k_rope, x_lru, y_gate = jnp.split(z, cuts, axis=-1)
    c_out = mla_attention(c_q, c_kv, k_rope, positions, q_norm_g, w_q_up, kv_norm_g, w_kv_up)
    d_out = rg_lru_branch(x_lru, y_gate, conv_w, conv_b, wa, ba, wx, bx, lam)
    return jnp.concatenate([c_out, d_out], axis=-1) @ w_out

def channel_mixer(h, up, conv_w, conv_b, down):
    hid = causal_dwconv(h @ up, conv_w, conv_b)
    gate, val = jnp.split(hid, 2, axis=-1)
    return (jax.nn.gelu(gate, approximate=True) * val) @ down

def first_inputs(seed: int = 0) -> dict:
    key = jax.random.key(seed)
    keys = iter(jax.random.split(key, 40))

    def dense(shape, fan_in):
        return jax.random.normal(next(keys), shape, jnp.float32) * (fan_in ** -0.5)

    def gain(shape):
        return 1.0 + 0.05 * jax.random.normal(next(keys), shape, jnp.float32)

    def small(shape, s=0.02):
        return s * jax.random.normal(next(keys), shape, jnp.float32)

    x = jax.random.normal(next(keys), (BATCH, SEQ, D_MODEL), jnp.float32)
    offset = jax.random.randint(next(keys), (BATCH, 1), 0, 64) * CHUNK
    positions = (offset + jnp.arange(SEQ)[None, :]).astype(jnp.int32)
    u = jax.random.uniform(next(keys), (N_ODD, LRU_WIDTH), jnp.float32, 0.9, 0.999)
    s = u ** (1.0 / LRU_C)
    lru_lambda = jnp.log(s) - jnp.log1p(-s)
    bw = LRU_WIDTH // LRU_BLOCKS
    return {
        'x': x,
        'positions': positions,
        'mix_pre_g': gain((DEPTH, D_MODEL)),
        'mix_post_g': gain((DEPTH, D_MODEL)),
        'ffn_pre_g': gain((DEPTH, D_MODEL)),
        'ffn_post_g': gain((DEPTH, D_MODEL)),
        'ffn_up': dense((DEPTH, D_MODEL, 2 * D_FF), D_MODEL),
        'ffn_conv_w': dense((DEPTH, FFN_CONV, 2 * D_FF), FFN_CONV),
        'ffn_conv_b': small((DEPTH, 2 * D_FF)),
        'ffn_down': dense((DEPTH, D_FF, D_MODEL), D_FF),
        'ab_w_in': dense((N_EVEN, D_MODEL, AB_IN), D_MODEL),
        'pool_w': dense((N_EVEN, len(POOL_WINDOWS), POOL_GROUP, POOL_GROUP), POOL_GROUP),
        'pool_b': small((N_EVEN, len(POOL_WINDOWS), POOL_GROUP)),
        'pool_scale': 1.0 + 0.1 * jax.random.normal(next(keys), (N_EVEN, POOL_WIDTH), jnp.float32),
        'ab_w_out': dense((N_EVEN, AB_OUT, D_MODEL), AB_OUT),
        'cd_w_in': dense((N_ODD, D_MODEL, CD_IN), D_MODEL),
        'q_norm_g': gain((N_ODD, Q_LORA)),
        'w_q_up': dense((N_ODD, Q_LORA, C_HEADS * (QK_NOPE + QK_ROPE)), Q_LORA),
        'kv_norm_g': gain((N_ODD, KV_LORA)),
        'w_kv_up': dense((N_ODD, KV_LORA, C_HEADS * (QK_NOPE + V_HEAD)), KV_LORA),
        'lru_conv_w': dense((N_ODD, LRU_CONV, LRU_WIDTH), LRU_CONV),
        'lru_conv_b': small((N_ODD, LRU_WIDTH)),
        'lru_wa': dense((N_ODD, LRU_BLOCKS, bw, bw), bw),
        'lru_ba': small((N_ODD, LRU_WIDTH), 0.1),
        'lru_wx': dense((N_ODD, LRU_BLOCKS, bw, bw), bw),
        'lru_bx': small((N_ODD, LRU_WIDTH), 0.1),
        'lru_lambda': lru_lambda,
        'cd_w_out': dense((N_ODD, CD_OUT, D_MODEL), CD_OUT),
    }

def first_block(x, positions, mix_pre_g, mix_post_g, ffn_pre_g, ffn_post_g,
              ffn_up, ffn_conv_w, ffn_conv_b, ffn_down,
              ab_w_in, pool_w, pool_b, pool_scale, ab_w_out,
              cd_w_in, q_norm_g, w_q_up, kv_norm_g, w_kv_up,
              lru_conv_w, lru_conv_b, lru_wa, lru_ba, lru_wx, lru_bx, lru_lambda, cd_w_out):
    for layer in range(DEPTH):
        j = layer // 2
        h = rms_norm(x, mix_pre_g[layer])
        if layer % 2 == 0:
            m = mixer_ab(h, ab_w_in[j], pool_w[j], pool_b[j], pool_scale[j], ab_w_out[j])
        else:
            m = mixer_cd(h, positions, cd_w_in[j], q_norm_g[j], w_q_up[j], kv_norm_g[j], w_kv_up[j],
                         lru_conv_w[j], lru_conv_b[j], lru_wa[j], lru_ba[j], lru_wx[j], lru_bx[j],
                         lru_lambda[j], cd_w_out[j])
        x = x + rms_norm(m, mix_post_g[layer])
        h = rms_norm(x, ffn_pre_g[layer])
        f = channel_mixer(h, ffn_up[layer], ffn_conv_w[layer], ffn_conv_b[layer], ffn_down[layer])
        x = x + rms_norm(f, ffn_post_g[layer])
    return x


D_MIX = D_MODEL
N_GROUPS = 4
GROUP_W = D_MIX // N_GROUPS
HEAD_DIM = 128
N_HEADS = GROUP_W // HEAD_DIM
DIFF_QK_DIM = HEAD_DIM // 2
MOBA_BLOCK = 256
MOBA_TOPK = 3
MOBA_Q_CHUNK = 64
GLA_DK = HEAD_DIM // 2
GLA_DV = HEAD_DIM
GLA_RANK = 16
GLA_TAU = 16.0
GLA_CHUNK = 64
ROPE_THETA_2 = 500000.0
ROPE_FRACTION = 4
RMS_EPS = 1e-6
FOX_F_BIAS_CENTER = 3.0

SEGMENTS = (
    ("fox_q", GROUP_W), ("fox_k", GROUP_W), ("fox_v", GROUP_W),
    ("fox_f", N_HEADS), ("fox_g", GROUP_W),
    ("diff_q", GROUP_W), ("diff_k", GROUP_W), ("diff_v", GROUP_W), ("diff_g", GROUP_W),
    ("moba_q", GROUP_W), ("moba_k", GROUP_W), ("moba_v", GROUP_W), ("moba_g", GROUP_W),
    ("gla_q", N_HEADS * GLA_DK), ("gla_k", N_HEADS * GLA_DK), ("gla_v", N_HEADS * GLA_DV),
    ("gla_a", GLA_RANK), ("gla_g", GROUP_W),
)
D_IN = sum(w for _, w in SEGMENTS)


def rms_norm_2(x, g):
    xf = x.astype(jnp.float32)
    y = xf * lax.rsqrt(jnp.mean(xf * xf, axis=-1, keepdims=True) + RMS_EPS)
    return (y * g.astype(jnp.float32)).astype(x.dtype)

def split_columns(proj):
    parts, off = {}, 0
    for name, width in SEGMENTS:
        parts[name] = proj[..., off:off + width]
        off += width
    return parts

def to_heads(t, d):
    b, s, _ = t.shape
    return t.reshape(b, s, -1, d).transpose(0, 2, 1, 3)

def from_heads(t):
    b, h, s, d = t.shape
    return t.transpose(0, 2, 1, 3).reshape(b, s, h * d)

def diff_pair(t):
    b, s, _ = t.shape
    t = t.reshape(b, s, N_HEADS, 2, DIFF_QK_DIM).transpose(3, 0, 2, 1, 4)
    return t[0], t[1]

def query_blocks(t, block):
    b, h, s, d = t.shape
    return t.reshape(b, h, s // block, block, d).transpose(2, 0, 1, 3, 4)

def merge_query_blocks(o):
    n, b, h, blk, d = o.shape
    return o.transpose(1, 2, 0, 3, 4).reshape(b, h, n * blk, d)

def rope_table(seq, rot_dim):
    inv_freq = ROPE_THETA_2 ** (-jnp.arange(0, rot_dim, 2, dtype=jnp.float32) / rot_dim)
    ang = jnp.arange(seq, dtype=jnp.float32)[:, None] * inv_freq[None, :]
    return jnp.cos(ang), jnp.sin(ang)

def partial_rope(t, cos, sin):
    half = cos.shape[-1]
    rot = 2 * half
    t1, t2, rest = t[..., :half], t[..., half:rot], t[..., rot:]
    c = cos.astype(t.dtype)
    s = sin.astype(t.dtype)
    return jnp.concatenate([t1 * c - t2 * s, t1 * s + t2 * c, rest], axis=-1)

def forgetting_attention(q, k, v, log_f):
    b, h, s_len, d = q.shape
    cum = jnp.cumsum(log_f.astype(jnp.float32), axis=-1)
    n_blk = s_len // Q_BLOCK
    cum_blocks = cum.reshape(b, h, n_blk, Q_BLOCK).transpose(2, 0, 1, 3)
    k_pos = jnp.arange(s_len)
    scale = d ** -0.5

    def block(args):
        i, q_i, c_i = args
        logits = jnp.einsum("bhqd,bhkd->bhqk", q_i, k, preferred_element_type=jnp.float32) * scale
        logits = logits + c_i[..., :, None] - cum[:, :, None, :]
        q_pos = i * Q_BLOCK + jnp.arange(Q_BLOCK)
        logits = jnp.where(k_pos[None, :] <= q_pos[:, None], logits, -jnp.inf)
        p = jax.nn.softmax(logits, axis=-1)
        return jnp.einsum("bhqk,bhkd->bhqd", p.astype(v.dtype), v)

    out = lax.map(block, (jnp.arange(n_blk), query_blocks(q, Q_BLOCK), cum_blocks))
    return merge_query_blocks(out)

def differential_attention(q1, q2, k1, k2, v, lam):
    s_len, d = q1.shape[2], q1.shape[3]
    n_blk = s_len // Q_BLOCK
    k_pos = jnp.arange(s_len)
    scale = d ** -0.5

    def block(args):
        i, q1_i, q2_i = args
        q_pos = i * Q_BLOCK + jnp.arange(Q_BLOCK)
        causal = k_pos[None, :] <= q_pos[:, None]

        def probs(q_i, k_full):
            logits = jnp.einsum("bhqd,bhkd->bhqk", q_i, k_full, preferred_element_type=jnp.float32) * scale
            return jax.nn.softmax(jnp.where(causal, logits, -jnp.inf), axis=-1)

        p = probs(q1_i, k1) - lam * probs(q2_i, k2)
        return jnp.einsum("bhqk,bhkd->bhqd", p.astype(v.dtype), v)

    out = lax.map(block, (jnp.arange(n_blk), query_blocks(q1, Q_BLOCK), query_blocks(q2, Q_BLOCK)))
    return merge_query_blocks(out)

def moba_attention(q, k, v):
    b, h, s_len, d = q.shape
    n_blk = -(-s_len // MOBA_BLOCK)
    pad = n_blk * MOBA_BLOCK - s_len
    widths = ((0, 0), (0, 0), (0, pad), (0, 0))
    qp, kp, vp = (jnp.pad(t, widths) for t in (q, k, v))
    k_blocks = kp.reshape(b, h, n_blk, MOBA_BLOCK, d)
    v_blocks = vp.reshape(b, h, n_blk, MOBA_BLOCK, d)
    k_mean = jnp.mean(k_blocks.astype(jnp.float32), axis=3)
    n_sel = min(MOBA_TOPK, n_blk)
    scale = d ** -0.5
    gather = jax.vmap(jax.vmap(lambda blocks, idx: blocks[idx]))

    def chunk(args):
        c, q_c = args
        q_pos = c * MOBA_Q_CHUNK + jnp.arange(MOBA_Q_CHUNK)
        own = (c * MOBA_Q_CHUNK) // MOBA_BLOCK
        gate = jnp.einsum("bhqd,bhnd->bhqn", q_c.astype(jnp.float32), k_mean)
        gate = jnp.where(jnp.arange(n_blk) < own, gate, -jnp.inf)
        _, top_idx = lax.top_k(gate, n_sel)
        sel_ok = jnp.arange(n_sel) < own
        k_sel = gather(k_blocks, top_idx)
        v_sel = gather(v_blocks, top_idx)
        s_sel = jnp.einsum("bhqd,bhqjld->bhqjl", q_c, k_sel, preferred_element_type=jnp.float32) * scale
        s_sel = jnp.where(sel_ok[:, None], s_sel, -jnp.inf).reshape(b, h, MOBA_Q_CHUNK, n_sel * MOBA_BLOCK)
        k_own = lax.dynamic_slice_in_dim(kp, own * MOBA_BLOCK, MOBA_BLOCK, axis=2)
        v_own = lax.dynamic_slice_in_dim(vp, own * MOBA_BLOCK, MOBA_BLOCK, axis=2)
        s_own = jnp.einsum("bhqd,bhld->bhql", q_c, k_own, preferred_element_type=jnp.float32) * scale
        own_pos = own * MOBA_BLOCK + jnp.arange(MOBA_BLOCK)
        s_own = jnp.where(own_pos[None, :] <= q_pos[:, None], s_own, -jnp.inf)
        p = jax.nn.softmax(jnp.concatenate([s_sel, s_own], axis=-1), axis=-1).astype(v.dtype)
        p_sel = p[..., :n_sel * MOBA_BLOCK].reshape(b, h, MOBA_Q_CHUNK, n_sel, MOBA_BLOCK)
        p_own = p[..., n_sel * MOBA_BLOCK:]
        return (jnp.einsum("bhqjl,bhqjld->bhqd", p_sel, v_sel)
                + jnp.einsum("bhql,bhld->bhqd", p_own, v_own))

    n_chunk = (n_blk * MOBA_BLOCK) // MOBA_Q_CHUNK
    out = lax.map(chunk, (jnp.arange(n_chunk), query_blocks(qp, MOBA_Q_CHUNK)))
    return merge_query_blocks(out)[:, :, :s_len]

def gla_chunked(q, k, v, log_a):
    b, h, s_len, dk = q.shape
    dv = v.shape[-1]
    qf = q.astype(jnp.float32) * dk ** -0.5
    kf = k.astype(jnp.float32)
    vf = v.astype(jnp.float32)
    gf = log_a.astype(jnp.float32)
    qc, kc, vc, gc = (query_blocks(t, GLA_CHUNK) for t in (qf, kf, vf, gf))
    causal = jnp.tril(jnp.ones((GLA_CHUNK, GLA_CHUNK), dtype=bool))[..., None]

    def step(state, inp):
        q_i, k_i, v_i, g_i = inp
        cum = jnp.cumsum(g_i, axis=2)
        rel = jnp.where(causal, cum[:, :, :, None, :] - cum[:, :, None, :, :], -jnp.inf)
        scores = jnp.einsum("bhtd,bhsd,bhtsd->bhts", q_i, k_i, jnp.exp(rel))
        o = (jnp.einsum("bhts,bhsv->bhtv", scores, v_i)
             + jnp.einsum("bhtd,bhdv->bhtv", q_i * jnp.exp(cum), state))
        last = cum[:, :, -1:, :]
        state = (jnp.exp(last[:, :, 0, :])[..., None] * state
                 + jnp.einsum("bhsd,bhsv->bhdv", k_i * jnp.exp(last - cum), v_i))
        return state, o

    state0 = jnp.zeros((b, h, dk, dv), jnp.float32)
    _, out = lax.scan(step, state0, (qc, kc, vc, gc))
    return merge_query_blocks(out).astype(v.dtype)

def hybrid_layer(x, layer_idx, norm_g, w_in, fox_fb, diff_lam, diff_norm_g,
                 gla_wa2, gla_ba, gla_norm_g, w_out, rope_diff, rope_moba):
    h = rms_norm_2(x, norm_g)
    p = split_columns(jnp.einsum("bsd,de->bse", h, w_in))

    log_f = jax.nn.log_sigmoid((p["fox_f"] + fox_fb).astype(jnp.float32)).transpose(0, 2, 1)
    fox = forgetting_attention(to_heads(p["fox_q"], HEAD_DIM), to_heads(p["fox_k"], HEAD_DIM),
                               to_heads(p["fox_v"], HEAD_DIM), log_f)
    fox = from_heads(fox) * jax.nn.silu(p["fox_g"])

    lambda_init = 0.8 - 0.6 * math.exp(-0.3 * layer_idx)
    lf = diff_lam.astype(jnp.float32)
    lam = jnp.exp(jnp.sum(lf[0] * lf[1])) - jnp.exp(jnp.sum(lf[2] * lf[3])) + lambda_init
    q1, q2 = diff_pair(p["diff_q"])
    k1, k2 = diff_pair(p["diff_k"])
    q1, q2, k1, k2 = (partial_rope(t, *rope_diff) for t in (q1, q2, k1, k2))
    diff = differential_attention(q1, q2, k1, k2, to_heads(p["diff_v"], HEAD_DIM), lam)
    diff = rms_norm_2(diff, diff_norm_g) * (1.0 - lambda_init)
    diff = from_heads(diff) * jax.nn.silu(p["diff_g"])

    mq = partial_rope(to_heads(p["moba_q"], HEAD_DIM), *rope_moba)
    mk = partial_rope(to_heads(p["moba_k"], HEAD_DIM), *rope_moba)
    moba = moba_attention(mq, mk, to_heads(p["moba_v"], HEAD_DIM))
    moba = from_heads(moba) * jax.nn.silu(p["moba_g"])

    a_logit = jnp.einsum("bsr,re->bse", p["gla_a"], gla_wa2) + gla_ba
    log_a = jax.nn.log_sigmoid(a_logit.astype(jnp.float32)) / GLA_TAU
    gla = gla_chunked(to_heads(p["gla_q"], GLA_DK), to_heads(p["gla_k"], GLA_DK),
                      to_heads(p["gla_v"], GLA_DV), to_heads(log_a, GLA_DK))
    gla = from_heads(rms_norm_2(gla, gla_norm_g)) * jax.nn.silu(p["gla_g"])

    mixed = jnp.concatenate([fox, diff, moba, gla], axis=-1)
    return x + jnp.einsum("bse,ed->bsd", mixed, w_out)

def second_inputs(seed: int = 0) -> dict:
    key = jax.random.key(seed)
    ks = jax.random.split(key, 11)
    f32 = jnp.float32
    nrm = jax.random.normal
    x = nrm(ks[0], (BATCH, SEQ, D_MODEL), f32)
    norm_g = 1.0 + 0.02 * nrm(ks[1], (DEPTH, D_MODEL), f32)
    w_in = nrm(ks[2], (DEPTH, D_MODEL, D_IN), f32) * D_MODEL ** -0.5
    fox_fb = FOX_F_BIAS_CENTER + 0.1 * nrm(ks[3], (DEPTH, N_HEADS), f32)
    diff_lam = 0.1 * nrm(ks[4], (DEPTH, 4, DIFF_QK_DIM), f32)
    diff_norm_g = 1.0 + 0.02 * nrm(ks[5], (DEPTH, HEAD_DIM), f32)
    gla_wa2 = nrm(ks[6], (DEPTH, GLA_RANK, N_HEADS * GLA_DK), f32) * GLA_RANK ** -0.5
    gla_ba = 0.1 * nrm(ks[7], (DEPTH, N_HEADS * GLA_DK), f32)
    gla_norm_g = 1.0 + 0.02 * nrm(ks[8], (DEPTH, GLA_DV), f32)
    w_out = nrm(ks[9], (DEPTH, D_MIX, D_MODEL), f32) * D_MIX ** -0.5
    final_norm_g = 1.0 + 0.02 * nrm(ks[10], (D_MODEL,), f32)
    return {"x": x, "norm_g": norm_g, "w_in": w_in, "fox_fb": fox_fb, "diff_lam": diff_lam,
            "diff_norm_g": diff_norm_g, "gla_wa2": gla_wa2, "gla_ba": gla_ba,
            "gla_norm_g": gla_norm_g, "w_out": w_out, "final_norm_g": final_norm_g}

def second_block(x, norm_g, w_in, fox_fb, diff_lam, diff_norm_g, gla_wa2, gla_ba,
              gla_norm_g, w_out, final_norm_g):
    s_len = x.shape[1]
    rope_diff = rope_table(s_len, DIFF_QK_DIM // ROPE_FRACTION)
    rope_moba = rope_table(s_len, HEAD_DIM // ROPE_FRACTION)
    for l in range(DEPTH):
        x = hybrid_layer(x, l, norm_g[l], w_in[l], fox_fb[l], diff_lam[l], diff_norm_g[l],
                         gla_wa2[l], gla_ba[l], gla_norm_g[l], w_out[l], rope_diff, rope_moba)
    return rms_norm_2(x, final_norm_g)


def setup_inputs(seed=0):
    out = dict(first_inputs(seed))
    for name, value in second_inputs(seed + 1).items():
        if name != "x":
            out[name + "_2"] = value
    return out


def reference(
    x, positions, mix_pre_g, mix_post_g, ffn_pre_g, ffn_post_g, ffn_up, ffn_conv_w, ffn_conv_b,
    ffn_down, ab_w_in, pool_w, pool_b, pool_scale, ab_w_out, cd_w_in, q_norm_g, w_q_up,
    kv_norm_g, w_kv_up, lru_conv_w, lru_conv_b, lru_wa, lru_ba, lru_wx, lru_bx, lru_lambda,
    cd_w_out, norm_g_2, w_in_2, fox_fb_2, diff_lam_2, diff_norm_g_2, gla_wa2_2, gla_ba_2,
    gla_norm_g_2, w_out_2, final_norm_g_2,
):
    x = first_block(
        x, positions, mix_pre_g, mix_post_g, ffn_pre_g, ffn_post_g, ffn_up, ffn_conv_w,
        ffn_conv_b, ffn_down, ab_w_in, pool_w, pool_b, pool_scale, ab_w_out, cd_w_in, q_norm_g,
        w_q_up, kv_norm_g, w_kv_up, lru_conv_w, lru_conv_b, lru_wa, lru_ba, lru_wx, lru_bx,
        lru_lambda, cd_w_out,
    )
    return second_block(
        x, norm_g_2, w_in_2, fox_fb_2, diff_lam_2, diff_norm_g_2, gla_wa2_2, gla_ba_2,
        gla_norm_g_2, w_out_2, final_norm_g_2,
    )


_drawn_inputs = setup_inputs


def setup_inputs(seed=0):
    import zlib

    import numpy as np

    out = dict(_drawn_inputs(seed))
    spreads = {}
    factors = {'q_norm_g': 4.454,
     'kv_norm_g': 3.309,
     'lru_ba': 5.176,
     'norm_g_2': 4.965,
     'fox_fb_2': 64.0,
     'diff_lam_2': 8.0,
     'diff_norm_g_2': 8.0,
     'gla_ba_2': 7.293,
     'gla_norm_g_2': 8.0,
     'final_norm_g_2': 7.681}
    for name, (base, spread) in spreads.items():
        noise = np.random.default_rng([zlib.crc32(name.encode()), seed]).standard_normal(out[name].shape)
        drawn = base * np.exp(spread * noise) if base else spread * noise
        out[name] = jnp.asarray(drawn.astype(out[name].dtype))
    for name, factor in factors.items():
        out[name] = (out[name] * factor).astype(out[name].dtype)
    return out
```

```python
import concourse.bass as bass
from concourse import mybir
from contextlib import ExitStack
import numpy as np

P = 128
T = 256
KT = 16
D_MODEL = KT * P
UB = 8
RAW = 4
SPLIT = 4
BANKS = 4
FF_T = 32
EPS = 1e-6
NEG = -1.0e30
TAKEN = -3.0e38
K_TOP = 64

VEC = [("mix_pre", 32), ("mix_post", 32), ("ffn_pre", 32), ("ffn_post", 32), ("norm2", 32), ("final", 16),
       ("q_norm", 4), ("kv_norm", 2), ("ffn_w", 2 * 3 * 64), ("ffn_b", 2 * 64), ("pool_b", 8),
       ("pool_scale", 8), ("lru_w", 32), ("lru_b", 8), ("lru_ba", 8), ("lru_bx", 8), ("lru_lam", 8),
       ("fox_fb", 2), ("diff_norm", 2), ("gla_norm", 2), ("gla_ba", 4), ("diff_lam", 8), ("gla_wa2", 512)]
TAB = [("ident", 128), ("ones", 256), ("chunk", 256), ("causal", 256), ("diff_cos", 256), ("diff_sin", 256),
       ("moba_cos", 256), ("moba_sin", 256), ("diff_rot", 128), ("moba_rot", 128), ("mla_rot", 128),
       ("freq", 1), ("pool_inv", 64), ("gla_mask", 192), ("head_row", 512)]


def offsets(parts):
    at, out = 0, {}
    for name, width in parts:
        out[name] = at
        at += width
    out["all"] = at
    return out


VO, TO = offsets(VEC), offsets(TAB)

AB_QI, AB_MISC, AB_Q, AB_K, AB_U, AB_V, AB_WI = 0, 8, 9, 17, 25, 33, 33
AB_POOL, AB_SEL, AB_ACC, AB_KI = 42, 58, 60, 62
CD_CQ, CD_CKV, CD_KR, CD_XL, CD_YG = 0, 4, 6, 7, 56
CD_XHI, CD_XLO, CD_GR, CD_GI = 24, 32, 40, 48
CD_NHI, CD_NLO, CD_QN, CD_QR, CD_KN, CD_V = 7, 13, 20, 28, 32, 40
CD_KRZ, CD_COS, CD_SIN = 48, 50, 51
Z_FQ, Z_FK, Z_DQ, Z_DK, Z_MQ, Z_MK, Z_MISC, Z_GQ, Z_GK, Z_G, Z_V = 0, 4, 8, 12, 16, 20, 24, 25, 27, 29, 45


class Engine:
    def __init__(self, load_tables, square_sum_x, rstd, norm_in, run, meet,
                 index, windows, attend, pool, post_norm, conv, lru, states, mla_norm, lru_out, mla,
                 rotate, log_gates, take_gla, head_norm, gla, finish):
        self.load_tables = load_tables
        self.square_sum_x = square_sum_x
        self.rstd = rstd
        self.norm_in = norm_in
        self.run = run
        self.meet = meet
        self.index = index
        self.windows = windows
        self.attend = attend
        self.pool = pool
        self.post_norm = post_norm
        self.conv = conv
        self.lru = lru
        self.states = states
        self.mla_norm = mla_norm
        self.lru_out = lru_out
        self.mla = mla
        self.rotate = rotate
        self.log_gates = log_gates
        self.take_gla = take_gla
        self.head_norm = head_norm
        self.gla = gla
        self.finish = finish


def program(nc, xT, pos, w, vec, tab, out, n_units):
    f32, f32r, i32 = mybir.dt.float32, mybir.dt.float32r, mybir.dt.int32
    ALU, ACT, AX = mybir.AluOpType, mybir.ActivationFunctionType, mybir.AxisListType
    ctx = ExitStack()
    with ctx:
        def sb(name, shape, dt=f32):
            return ctx.enter_context(nc.sbuf_tensor(name, shape, dt))

        with nc.sbuf_tensor("BIGR", [P, 64, T], f32r) as BIGR:
            pass
        BIG = sb("BIG", [P, 64, T])
        X = sb("X", [P, KT, T])
        HHI, HLO = sb("HHI", [P, KT, T], f32r), sb("HLO", [P, KT, T], f32r)
        M = sb("M", [P, KT, T])
        RING = [sb(f"RING{s}", [P, UB * P]) for s in range(RAW)]
        WHI = [sb(f"WHI{s}", [P, UB, P], f32r) for s in range(SPLIT)]
        WLO = [sb(f"WLO{s}", [P, UB, P], f32r) for s in range(SPLIT)]
        V = sb("V", [P, VO["all"]])
        TB = sb("TB", [P, TO["all"]])
        TM = sb("TM", [P, 12, T])
        SMALL = sb("SMALL", [P, 64])
        POS = sb("POS", [P, T], i32)
        BANK = [ctx.enter_context(nc.psum_tensor(f"BANK{b}", [P, 512], f32)) for b in range(8)]

        sems = {}

        def sem(name):
            if name not in sems:
                sems[name] = ctx.enter_context(nc.semaphore(name))
            return sems[name]

        def vcol(name, c):
            return V[:, bass.ds(c + VO[name], 1)]

        def tcol(name, n, at=0):
            return TB[:, TO[name] + at:TO[name] + at + n]

        ident, ones = tcol("ident", P), tcol("ones", P)

        def step_no(counts, name, n=1):
            counts[name] = counts.get(name, 0) + n
            return counts[name]

        class Run:
            def __init__(self, n, blocks, form, src, kind, dst=0, last=False):
                self.n, self.blocks, self.form, self.src = n, blocks, form, src
                self.kind, self.dst, self.last = kind, dst, last
                self.units = n * blocks // UB

        FFN = {l: [Run(64, KT, "f", "H", "ffn", l), Run(16, FF_T, "f", "HID", "m")] for l in (0, 1)}
        RUNS_INDEX = [Run(9, KT, "f", "H", "f", AB_QI), Run(2, KT, "v", "H", "v", AB_WI)]
        RUN_QKU, RUN_V = Run(24, KT, "f", "H", "f", AB_Q), Run(8, KT, "v", "H", "v", AB_V)
        RUN_MIX = Run(16, KT, "f", "H", "m")
        RUN_X, RUN_C, RUN_Y = (Run(n, KT, "f", "H", "f", at) for n, at in ((8, CD_XL), (7, CD_CQ), (8, CD_YG)))
        RUNS_2 = [Run(21, KT, "f", "H", "f", Z_MISC), Run(16, KT, "v", "H", "v", Z_V)]
        RUN_FOX_DIFF, RUN_MOBA = Run(16, KT, "f", "H", "f", Z_FQ), Run(8, KT, "f", "H", "f", Z_MQ)
        RUN_ADD = Run(16, KT, "f", "H", "add")
        RUN_END = Run(16, KT, "f", "H", "add", last=True)

        def schedule(e):
            e.load_tables()
            e.square_sum_x(first=True)
            e.rstd(D_MODEL)
            e.norm_in("mix_pre", 0)
            for r in RUNS_INDEX:
                e.run(r)
            e.run(RUN_QKU, e.index)
            e.windows()
            e.run(RUN_V)
            e.meet()
            e.attend("dsa")
            e.meet()
            e.pool()
            e.meet()
            e.run(RUN_MIX)
            e.post_norm("mix_post", 0)
            e.rstd(D_MODEL)
            e.norm_in("ffn_pre", 0)
            for r in FFN[0]:
                e.run(r)
            e.post_norm("ffn_post", 0)
            e.rstd(D_MODEL)
            e.norm_in("mix_pre", 1)
            e.run(RUN_X)
            e.run(RUN_C, e.conv)
            e.lru()
            e.run(RUN_Y, e.states)
            e.meet()
            e.mla_norm()
            e.lru_out()
            e.mla()
            e.meet()
            e.attend("mla")
            e.meet()
            e.run(RUN_MIX)
            e.post_norm("mix_post", 1)
            e.rstd(D_MODEL)
            e.norm_in("ffn_pre", 1)
            for r in FFN[1]:
                e.run(r)
            e.post_norm("ffn_post", 1)
            for l in (0, 1):
                if l:
                    e.square_sum_x()
                e.rstd(D_MODEL)
                e.norm_in("norm2", l)
                for r in RUNS_2:
                    e.run(r)
                e.run(RUN_FOX_DIFF, e.gla, l)
                e.run(RUN_MOBA, e.log_gates, l)
                e.meet()
                e.rotate(l)
                e.take_gla()
                e.meet()
                e.attend("fox", l)
                e.meet()
                e.attend("moba", l)
                e.meet()
                e.attend("diff", l)
                e.meet()
                e.head_norm("diff", l)
                e.meet()
                e.run(RUN_END if l else RUN_ADD)
                e.meet()
            e.square_sum_x()
            e.rstd(D_MODEL)
            e.finish()

        def big(k, lo=0, hi=T):
            return BIG[:, k, lo:hi]

        def table_mask(name):
            return lambda h, t: tcol(name, T)[:, P:T] if t == 0 else tcol(name, T)

        def tokens(at, n):
            return BIG[:, at:at + n, :].rearrange("p a b -> p (a b)").rearrange("p (s c) -> p s c", s=2)

        class Attention:
            def __init__(self, kind):
                self.kind, self.sets = kind, 2 if kind == "diff" else 1
                self.heads = 8 if kind in ("dsa", "mla") else 4
                self.out = {"dsa": 0, "mla": 0, "fox": 0, "diff": 4, "moba": 8}[kind]
                self.scale = {"mla": (P + 64) ** -0.5, "diff": 64 ** -0.5}.get(kind, P ** -0.5)
                self.mask = {"dsa": lambda h, t: big(AB_SEL + t, 0, P * (t + 1)), "mla": table_mask("chunk"),
                             "fox": lambda h, t: M[:, 2 * h + t, 0:P * (t + 1)]}.get(kind, table_mask("causal"))
                at, n, skip = {"dsa": (AB_V, 8, 0), "mla": (CD_V, 8, 0)}.get(kind, (Z_V, 16, self.out))
                self.value = lambda s, h: tokens(at, n)[:, s, (skip + h) * P:(skip + h + 1) * P]
                self.gated = kind in ("fox", "moba")
                self.items = [(h, t) for h in range(self.heads) for t in (0, 1)]

            def operands(self, h, t, j):
                q, k = slice(t * P, (t + 1) * P), slice(0, P * (t + 1))
                if self.kind == "mla":
                    return [(BIG[:, CD_QN + h, q], BIG[:, CD_KN + h, k]),
                            (BIG[:, CD_QR + h // 2, q], BIG[:, CD_KRZ + h % 2, k])]
                if self.kind == "diff":
                    return [(BIG[:, Z_DQ + h, q], M[:, 8 + 4 * j + h, k])]
                a, b = {"dsa": (AB_Q, AB_K), "fox": (Z_FQ, Z_FK), "moba": (Z_MQ, Z_MK)}[self.kind]
                return [(BIG[:, a + h, q], BIG[:, b + h, k])]

        def score(n, j, W):
            return TM[:, 2 * (n % 2) + j, 0:W]

        def turned(h):
            return TM[:, 4 + 2 * (h % 2):6 + 2 * (h % 2), :]

        def head_out(h):
            return TM[:, 8 + h % 2, :]

        NEG_MAX, SUMS, RECIPS, NEG_LAM, LAM_E, TOP8, LRU_C, FOX_F, SM = 0, 4, 8, 12, 14, 16, 24, 32, 40

        def small(at, n=1):
            return SMALL[:, at:at + n]

        class Short:
            def __init__(self, n, blocks, form, hi, lo):
                self.n, self.blocks, self.form, self.hi, self.lo = n, blocks, form, hi, lo

            def ends_unit(self, m):
                return (m + 1) * self.blocks % UB == 0

        POOL_RUN = Short(8, 2, "f", lambda m, k: BIGR[:, AB_POOL + 2 * (m // 2) + k, :],
                         lambda m, k: BIGR[:, AB_POOL + 8 + 2 * (m // 2) + k, :])
        LRU_RUN = Short(16, 1, "f", lambda m, k: BIGR[:, CD_XHI + m % 8, :], lambda m, k: BIGR[:, CD_XLO + m % 8, :])
        Q_RUN = Short(12, 4, "f", lambda m, k: BIGR[:, CD_NHI + k, :], lambda m, k: BIGR[:, CD_NLO + k, :])
        KN_RUN = Short(8, 2, "f", lambda m, k: BIGR[:, CD_NHI + 4 + k, :], lambda m, k: BIGR[:, CD_NLO + 4 + k, :])
        KV_RUN = Short(8, 2, "v", KN_RUN.hi, KN_RUN.lo)

        MLA_ROPE = [(CD_QR + k, "mla_rot", big(CD_COS), big(CD_SIN)) for k in range(4)] + \
                   [(CD_KR, "mla_rot", big(CD_COS), big(CD_SIN))]
        ROPE_DIFF, ROPE_MOBA = [[(at + h, f"{kind}_rot", tcol(f"{kind}_cos", T), tcol(f"{kind}_sin", T))
                                 for at in tiles for h in range(4)]
                                for kind, tiles in (("diff", (Z_DQ, Z_DK)), ("moba", (Z_MQ, Z_MK)))]

        GLA_CUM, GLA_ST = 61, Z_MQ
        LEVELS = [128, 64, 32, 16, 8, 4, 2, 1, 0]
        CUM = BIG[:, GLA_CUM:GLA_CUM + 2, :]
        EXPS = M[:, 4:6, :].rearrange("p a b -> p (a b)")
        QQ = M[:, 6:8, :]
        KK = M[:, 8:12, :].rearrange("p (r i) t -> p r i t", r=2)
        ST = BIG[:, GLA_ST:GLA_ST + 8, :].rearrange("p (h s) t -> p h s t", h=4)
        DIAG, DIAG_NEW = M[:, 12, :], M[:, 13, :]

        def blocks(tile2, odd, B):
            return tile2.rearrange("p i (m e r) -> p i m e r", e=2, r=B)[:, :, :, odd, :]

        ENGINES = ("pe", "act", "dve", "pool")

        def meet(eng, me, c):
            n = step_no(c, "meet")
            eng.drain().then_inc(sem(f"{me}_met"), 1)
            for other in ENGINES:
                if other != me:
                    eng.wait_ge(sem(f"{other}_met"), n)

        def groups(eng, r, step, beside=None):
            if beside or r.n < BANKS:
                beside = beside or iter(())
                for m in range(r.n):
                    step(m // BANKS, m % BANKS)
                    next(beside, None)
                for _ in beside:
                    pass
                return
            full = r.n // BANKS - (1 if r.last else 0)
            for j in range(BANKS):
                step(0, j)
            if full > 1:
                with eng.Fori(1, full) as i:
                    for j in range(BANKS):
                        step(i, j)
            for m in range(full * BANKS, r.n):
                step(m // BANKS, m % BANKS)

        def whole(parts):
            for _ in parts:
                pass

        def begin(c, units, outputs):
            at = c.get("unit", 0), c.get("output", 0)
            c["unit"], c["output"] = at[0] + units, at[1] + outputs
            return at

        def least(i):
            return i if isinstance(i, int) else 1

        block = ctx.enter_context(nc.Block())

        @block.sync
        def _(sp):
            for u in range(RAW):
                sp.dma_start(RING[u][:, :], w[u]).then_inc(sem(f"loaded{u}"), 16)
            with sp.Fori(1, n_units // RAW) as i:
                for s in range(RAW):
                    sp.wait_ge(sem("lo_done"), i * RAW + s - (RAW - 1))
                    sp.dma_start(RING[s][:, :], w[i * RAW + s]).then_inc(sem(f"loaded{s}"), 16)
            for u in range(n_units // RAW * RAW, n_units):
                sp.wait_ge(sem("lo_done"), u - (RAW - 1))
                sp.dma_start(RING[u % RAW][:, :], w[u]).then_inc(sem(f"loaded{u % RAW}"), 16)
            sp.wait_ge(sem("lo_done"), n_units)
            for quarter in range(4):
                sp.wait_ge(sem("final"), 4 * (quarter + 1))
                sp.dma_start(out[:, 4 * quarter:4 * quarter + 4, :], M[:, 4 * quarter:4 * quarter + 4, :])\
                  .then_inc(sem("stored"), 16)
            sp.wait_ge(sem("stored"), 64)

        @block.tensor
        def _(pe):
            c = {}
            mm = nc.tensor.matmul

            def product(bank, s, kk, hi, lo, start, stop):
                for n, (wt, x) in enumerate([(WHI, hi), (WHI, lo), (WLO, hi)]):
                    last = mm(bank[:, 0:T], wt[s][:, kk, :], x, start=start and n == 0, stop=stop and n == 2)
                return last

            def product_v(pair, s, kk, hi, lo, start, stop):
                for t in (0, 1):
                    for n, (wt, x) in enumerate([(WHI, hi), (WLO, hi), (WHI, lo)]):
                        last = mm(pair[t][:, 0:T], x[:, t * P:(t + 1) * P],
                                  wt[s][:, kk:kk + 2, :].rearrange("p a b -> p (a b)"),
                                  start=start and n == 0, stop=stop and n == 2)
                return last

            def run(r, beside=None, l=0):
                u0, o0 = begin(c, r.units, r.n)
                upo = r.blocks // UB
                src = (lambda k: (HHI[:, k, :], HLO[:, k, :])) if r.src == "H" else \
                      (lambda k: (BIGR[:, k, :], BIGR[:, FF_T + k, :]))
                if r.src == "HID":
                    pe.wait_ge(sem("hid_lo"), step_no(c, "hid", FF_T))

                def step(i, j):
                    if r.form == "v":
                        if j % 2:
                            step_v(i, j)
                        return
                    o = i * BANKS + (o0 + j)
                    if not isinstance(i, int) or o >= BANKS:
                        pe.wait_ge(sem("bank_free"), o - (BANKS - 1))
                    for h in range(upo):
                        at = u0 + j * upo + h
                        pe.wait_ge(sem("lo_done"), i * (BANKS * upo) + (at + 1))
                        for kk in range(UB):
                            k = h * UB + kk
                            if c.get("normed") is not None and isinstance(i, int) and i == 0 and j == 0:
                                pe.wait_ge(sem("normed_lo"), c["normed"] + k + 1)
                            last = product(BANK[(o0 + j) % BANKS], at % SPLIT, kk, *src(k),
                                           k == 0, k == r.blocks - 1)
                        last.then_inc(sem("unit_used"), 1)

                def step_v(i, j):
                    o = i * BANKS + (o0 + j)
                    if not isinstance(i, int) or o >= BANKS:
                        pe.wait_ge(sem("bank_free"), o - (BANKS - 1))
                    for h in range(2 * upo):
                        at = u0 + (j - 1) * upo + h
                        pe.wait_ge(sem("lo_done"), i * (BANKS * upo) + (at + 1))
                        for kk in range(0, UB, 2):
                            k = (h * UB + kk) // 2
                            last = product_v([BANK[(o0 + j - 1 + t) % BANKS] for t in (0, 1)], at % SPLIT, kk, *src(k),
                                             k == 0, k == r.blocks - 1)
                        last.then_inc(sem("unit_used"), 1)

                groups(pe, r, step, beside and beside(l, o0))
                c["normed"] = None

            def short(r):
                u0, o0 = begin(c, r.n * r.blocks // UB, r.n)
                for m in range(1, r.n, 2) if r.form == "v" else range(r.n):
                    pe.wait_ge(sem("bank_free"), o0 + m - (BANKS - 1))
                    if r.form == "v":
                        b0 = (m - 1) * r.blocks
                        if b0 % UB == 0:
                            pe.wait_ge(sem("lo_done"), u0 + b0 // UB + 1)
                        for k in range(r.blocks):
                            last = product_v([BANK[(o0 + m - 1 + t) % BANKS] for t in (0, 1)], (u0 + b0 // UB) % SPLIT,
                                             b0 % UB + 2 * k, r.hi(m, k), r.lo(m, k), k == 0, k == r.blocks - 1)
                        last.then_inc(sem("short_out"), 2)
                        if r.ends_unit(m):
                            pe.drain().then_inc(sem("unit_used"), 1)
                        continue
                    for k in range(r.blocks):
                        b = m * r.blocks + k
                        if b % UB == 0:
                            pe.wait_ge(sem("lo_done"), u0 + b // UB + 1)
                        last = product(BANK[(o0 + m) % BANKS], (u0 + b // UB) % SPLIT, b % UB,
                                       r.hi(m, k), r.lo(m, k), k == 0, k == r.blocks - 1)
                    last.then_inc(sem("short_out"), 1)
                    if r.ends_unit(m):
                        pe.drain().then_inc(sem("unit_used"), 1)

            def square_sum(n, x=None):
                for k in range(n):
                    pe.wait_ge(sem("squared"), step_no(c, "squared"))
                    mm(BANK[7][:, 0:T], ones, TM[:, k % 4, :], start=k == 0, stop=k == n - 1).then_inc(sem("summed"), 1)

            def post_norm(name, l):
                pe.wait_ge(sem("sq_added"), step_no(c, "sq_added", KT))
                mm(BANK[7][:, 0:T], ones, TM[:, 4, :], start=True, stop=True).then_inc(sem("summed"), 1)
                square_sum(KT)

            def norm_in(name, l):
                c["normed"] = c.get("norm_tiles", 0)
                c["norm_tiles"] = c["normed"] + KT

            def index(l, o0):
                pe.wait_ge(sem("bank_free"), o0)
                for n in range(32):
                    t, h = divmod(n, 16)
                    if n == 0:
                        pe.wait_ge(sem("keys_padded"), 1)
                    if n >= 4:
                        pe.wait_ge(sem("rectified"), n - 3)
                    mm(BANK[4 + n % 4][:, 0:P * (t + 1)], big(AB_QI + h // 2, t * P, (t + 1) * P),
                       big(AB_KI + h % 2, 0, P * (t + 1)), start=True, stop=True).then_inc(sem("logit"), 1)
                    if n % 4 == 3:
                        yield

            def attend(kind, l=0):
                a = Attention(kind)
                g0, h0 = c.get("item", 0), c.get("head", 0)
                N = len(a.items)
                c["item"], c["head"] = g0 + N, h0 + a.heads
                if kind == "diff":
                    pe.wait_ge(sem("keys_halved"), step_no(c, "keys_halved"))
                for n in range(N + 2):
                    if n < N:
                        h, t = a.items[n]
                        if g0 + n >= 2:
                            pe.wait_ge(sem("masked"), g0 + n - 1)
                        for j in range(a.sets):
                            parts = a.operands(h, t, j)
                            for i, (q, k) in enumerate(parts):
                                last = mm(BANK[4 + 2 * (n % 2) + j][:, 0:P * (t + 1)], q, k,
                                          start=i == 0, stop=i == len(parts) - 1)
                        last.then_inc(sem("scored"), 1)
                    if 0 <= n - 1 < N:
                        h, t = a.items[n - 1]
                        pe.wait_ge(sem("normalised"), g0 + n)
                        if g0 + n - 1 >= 2:
                            pe.wait_ge(sem("turned_out"), g0 + n - 2)
                        for s in range(t + 1):
                            last = nc.tensor.transpose(BANK[2 + (n - 1) % 2][:, s * P:(s + 1) * P],
                                                       score(n - 1, 0, T)[:, s * P:(s + 1) * P], ident)
                        last.then_inc(sem("turned"), 1)
                    if 0 <= n - 2 < N and a.items[n - 2][1] == 1:
                        h, _ = a.items[n - 2]
                        pe.wait_ge(sem("turned_out"), g0 + n - 1)
                        if h0 + h >= 2:
                            pe.wait_ge(sem("head_taken"), h0 + h - 1)
                        mm(BANK[h % 2][:, 0:T], a.value(0, h), turned(h)[:, 0, :], start=True, stop=False)
                        mm(BANK[h % 2][:, P:T], a.value(1, h), turned(h)[:, 1, P:T], start=False, stop=True)\
                            .then_inc(sem("head_done"), 1)

            def lru():
                pe.wait_ge(sem("conv_split"), 8)
                short(LRU_RUN)

            def rope(tiles):
                for n, (k, rot, _, _) in enumerate(tiles):
                    g = step_no(c, "rope") - 1
                    if n >= 2:
                        pe.wait_ge(sem("rope_read"), g - 1)
                    mm(BANK[4 + n % 2][:, 0:T], tcol(rot, P), big(k), start=True, stop=True).then_inc(sem("rope_done"), 1)
                    yield
                pe.wait_ge(sem("rope_read"), c["rope"])

            def mla_norm():
                square_sum(4)
                square_sum(2)
                pe.wait_ge(sem("normed_lo"), step_no(c, "norm_tiles", 6))

            def mla():
                short(Q_RUN)
                short(KN_RUN)
                short(KV_RUN)
                pe.wait_ge(sem("bank_free"), c["output"])
                whole(rope(MLA_ROPE))

            def decay_logits(l):
                mm(BANK[5][:, 0:T], V[0:16, VO["gla_wa2"] + 256 * l:VO["gla_wa2"] + 256 * l + P],
                   BIG[0:16, Z_MISC, :], start=True, stop=True)
                mm(BANK[5][:, T:2 * T], V[0:16, VO["gla_wa2"] + 256 * l + P:VO["gla_wa2"] + 256 * l + 2 * P],
                   BIG[0:16, Z_MISC, :], start=True, stop=True).then_inc(sem("decay_logit"), 1)

            def log_gates(l, o0):
                pe.wait_ge(sem("bank_free"), o0)
                pe.wait_ge(sem("head_mean"), c["head_norm"])
                turn = rope(ROPE_DIFF)
                next(turn)
                yield
                next(turn)
                pe.wait_ge(sem("forget_sum"), l + 1)
                for t in (0, 1):
                    last = mm(BANK[6][:, 4 * t:4 * t + 4], TM[32:36, 1, t * P:(t + 1) * P], ident[32:36, 32:36],
                              start=True, stop=True)
                last.then_inc(sem("forget_cols"), 1)
                yield
                for h in range(4):
                    next(turn)
                    if h == 1:
                        pe.wait_ge(sem("forget_taken"), l + 1)
                    if h >= 2:
                        pe.wait_ge(sem("fox_bias"), 4 * l + h - 1)
                    mm(BANK[7 - h % 2][:, 0:T], TB[32:36, TO["head_row"] + h * P:TO["head_row"] + (h + 1) * P],
                       TM[32:36, 1, :], start=True, stop=True).then_inc(sem("forget_rows"), 1)
                    yield
                next(turn)
                pe.wait_ge(sem("fox_bias"), 4 * l + 4)
                pe.wait_ge(sem("lam_products"), l + 1)
                mm(BANK[6][:, 0:2], ones[0:64, :], SMALL[0:64, LAM_E:LAM_E + 2], start=True, stop=True)\
                    .then_inc(sem("lam_summed"), 1)
                yield
                whole(turn)

            def head_norm(kind, l):
                n = step_no(c, "head_norm")
                pe.wait_ge(sem("head_squared"), n)
                for half in (0, 1):
                    last = mm(BANK[5 + half][:, :], ones, M[:, 4 + 2 * half:6 + 2 * half, :].rearrange("p a b -> p (a b)"),
                              start=True, stop=True)
                last.then_inc(sem("head_summed"), 1)

            def gla(l, o0):
                pe.wait_ge(sem("bank_free"), o0)
                decay_logits(l)
                yield
                yield
                for n, B in enumerate(LEVELS):
                    pe.wait_ge(sem("level_ready"), step_no(c, "level"))
                    for h in range(4):
                        ti, par = h // 2, h % 2
                        if B == 128:
                            last = mm(BANK[4][:, h * P:(h + 1) * P], KK[:, par, ti, 0:P], QQ[:, ti, P:T], start=True, stop=True)
                        elif B == 64:
                            for m in (0, 1):
                                last = mm(BANK[5][0:64, (2 * h + m) * 64:(2 * h + m + 1) * 64],
                                          KK[:, par, ti, m * P:m * P + 64], QQ[:, ti, m * P + 64:m * P + P],
                                          start=True, stop=True)
                        elif B == 32:
                            for m in range(4):
                                r = 64 * (m % 2)
                                last = mm(BANK[6][r:r + 32, (2 * h + m // 2) * 32:(2 * h + m // 2 + 1) * 32],
                                          KK[:, par, ti, 64 * m:64 * m + 32], QQ[:, ti, 64 * m + 32:64 * m + 64],
                                          start=True, stop=True)
                        else:
                            for j in range(8):
                                r = 32 * (j % 4)
                                last = mm(BANK[7][r:r + 32, (2 * h + j // 4) * 32:(2 * h + j // 4 + 1) * 32],
                                          KK[:, par, ti, 32 * j:32 * j + 32], QQ[:, ti, 32 * j:32 * j + 32],
                                          start=True, stop=True)
                    last.then_inc(sem("level_scored"), 1)
                    yield
                pe.wait_ge(sem("gla_scores"), l + 1)
                for h in range(4):
                    vals = tokens(Z_V, 16)
                    mm(BANK[4 + h % 2][:, (h // 2) * T:(h // 2 + 1) * T], vals[:, 0, (12 + h) * P:(13 + h) * P],
                       ST[:, h, 0, :], start=True, stop=False)
                    mm(BANK[4 + h % 2][:, (h // 2) * T + P:(h // 2 + 1) * T], vals[:, 1, (12 + h) * P:(13 + h) * P],
                       ST[:, h, 1, P:T], start=False, stop=True).then_inc(sem("gla_out"), 1)
                yield
                head_norm("gla", l)

            nothing = lambda *a, **k: None
            none_beside = lambda l, o0: iter(())
            schedule(Engine(
                load_tables=lambda: pe.wait_ge(sem("tables"), 64), square_sum_x=lambda first=False: square_sum(KT),
                rstd=nothing, norm_in=norm_in, run=run, meet=lambda: meet(pe, "pe", c), index=index,
                windows=nothing, attend=attend, pool=lambda: (pe.wait_ge(sem("pooled"), 1), short(POOL_RUN)),
                post_norm=post_norm, conv=none_beside, lru=lru, states=none_beside, mla_norm=mla_norm, lru_out=nothing,
                mla=mla, rotate=lambda l: whole(rope(ROPE_MOBA)), log_gates=log_gates, take_gla=nothing, head_norm=head_norm, gla=gla, finish=nothing))

        @block.scalar
        def _(act):
            c = {}
            A = nc.scalar.activation

            def high(at, i, per):
                if isinstance(i, int) and i * per + at >= n_units:
                    return
                act.wait_ge(sem(f"loaded{at % RAW}"), i * (per * 16 // RAW) + 16 * (at // RAW + 1))
                if least(i) * per + at >= SPLIT:
                    act.wait_ge(sem("unit_used"), i * per + (at - (SPLIT - 1)))
                A(WHI[at % SPLIT][:, :, :], RING[at % RAW][:, :].rearrange("p (k n) -> p k n", k=UB), ACT.Copy)\
                    .then_inc(sem("hi_done"), 1)

            def load_tables():
                act.dma_start(X[:, :, :], xT).then_inc(sem("tables"), 16)
                act.dma_start(V[:, :], vec).then_inc(sem("tables"), 16)
                act.dma_start(TB[:, :], tab).then_inc(sem("tables"), 16)
                act.dma_start(POS[:, :], pos).then_inc(sem("tables"), 16)
                for u in range(SPLIT):
                    high(u, 0, 0)
                act.wait_ge(sem("tables"), 64)

            def run(r, beside=None, l=0):
                u0, o0 = begin(c, r.units, r.n)
                upo = r.blocks // UB
                per = BANKS * upo
                if r.kind == "m":
                    g0 = c.get("m_outputs", 0)
                    c["m_outputs"] = g0 + r.n
                if r.kind == "ffn":
                    p0 = c.get("pairs", 0)
                    c["pairs"] = p0 + r.n // 2

                def step(i, j):
                    bank = BANK[(o0 + j) % BANKS]
                    for h in range(upo - 1):
                        high(u0 + SPLIT + j * upo + h, i, per)
                    if r.kind in ("f", "m") or r.kind == "v" and j % 2:
                        act.wait_ge(sem("unit_used"), i * per + (u0 + (j + 1) * upo))
                    if r.kind == "f":
                        A(BIG[:, i * BANKS + (r.dst + j), :], bank[:, 0:T], ACT.Copy).then_inc(sem("bank_free"), 1)
                    elif r.kind == "v" and j % 2:
                        for t in (0, 1):
                            A(tokens(r.dst, r.n)[:, t, bass.ds(i * (BANKS * P) + (j - 1) * P, 2 * P)],
                              BANK[(o0 + j - 1 + t) % BANKS][:, 0:T], ACT.Copy).then_inc(sem("bank_free"), 1)
                    elif r.kind == "m":
                        if least(i) * BANKS + g0 + j >= 4:
                            act.wait_ge(sem("sq_added"), i * BANKS + (g0 + j - 3))
                        A(TM[:, j, :], bank[:, 0:T], ACT.Square).then_inc(sem("sq_done"), 1)
                        A(M[:, i * BANKS + j, :], bank[:, 0:T], ACT.Copy).then_inc(sem("bank_free"), 1)
                    high(u0 + SPLIT + j * upo + upo - 1, i, per)
                    if r.kind == "ffn" and j % 2:
                        pair = i * 2 + (p0 + j // 2)
                        act.wait_ge(sem("bank_free"), i * BANKS + (o0 + j + 1))
                        if least(i) * 2 + p0 + j // 2 >= 2:
                            act.wait_ge(sem("gated"), pair - 1)
                        A(TM[:, 4 + j // 2, :], TM[:, j - 1, :], ACT.Gelu_apprx_tanh).then_inc(sem("gelu_done"), 1)

                groups(act, r, step, beside and beside(l, o0))

            def short(r, leave):
                u0, o0 = begin(c, r.n * r.blocks // UB, r.n)
                for m in range(r.n):
                    act.wait_ge(sem("short_out"), step_no(c, "short_out"))
                    leave(m, BANK[(o0 + m) % BANKS])
                    if r.ends_unit(m):
                        high(u0 + SPLIT + ((m + 1) * r.blocks // UB - 1), 0, 0)

            def square_sum(n, x, new=None):
                for k in range(n):
                    if new:
                        act.wait_ge(sem(new), step_no(c, new))
                    s = step_no(c, "squares")
                    if k >= 4:
                        act.wait_ge(sem("summed"), c["summed"] + k - 3)
                    A(TM[:, k % 4, :], x(k), ACT.Square).then_inc(sem("squared"), 1)
                c["summed"] += n

            c["summed"] = 0

            def rstd(width):
                n = step_no(c, "rstd")
                act.wait_ge(sem("mean_sq"), n)
                A(TM[:, 11, :], TM[:, 10, :], ACT.Sqrt).then_inc(sem("root"), 1)

            def normed(hi):
                for k, dst in enumerate(hi):
                    act.wait_ge(sem("normed"), step_no(c, "normed"))
                    A(dst, TM[:, 4 + k % 4, :], ACT.Copy).then_inc(sem("normed_hi"), 1)

            def post_norm(name, l):
                c["summed"] += 1
                rstd(D_MODEL)
                square_sum(KT, lambda k: X[:, k, :], "x_new")

            def index(l, o0):
                for n in range(32):
                    t = n // 16
                    act.wait_ge(sem("logit"), n + 1)
                    if n >= 4:
                        act.wait_ge(sem("weighed"), n - 3)
                    A(TM[:, n % 4, 0:P * (t + 1)], BANK[4 + n % 4][:, 0:P * (t + 1)], ACT.Relu, scale=1 / 32)\
                        .then_inc(sem("rectified"), 1)
                    if n % 4 == 3:
                        yield

            def attend(kind, l=0):
                a = Attention(kind)
                g0, h0 = c.get("item", 0), c.get("head", 0)
                N = len(a.items)
                c["item"], c["head"] = g0 + N, h0 + a.heads
                for n in range(N + 3):
                    if n < N:
                        h, t = a.items[n]
                        act.wait_ge(sem("maxed"), g0 + n + 1)
                        for j in range(a.sets):
                            W = P * (t + 1)
                            k = 2 * (n % 2) + j
                            last = A(score(n, j, W), score(n, j, W), ACT.Exp, bias=small(NEG_MAX + k),
                                     accum_out=small(SUMS + k))
                        last.then_inc(sem("powered"), 1)
                    if 0 <= n - 1 < N:
                        h, t = a.items[n - 1]
                        act.wait_ge(sem("turned"), g0 + n)
                        if t == 0 and h0 + h >= 2:
                            act.wait_ge(sem("head_done"), h0 + h - 1)
                        A(turned(h)[:, 0:t + 1, t * P:(t + 1) * P],
                          BANK[2 + (n - 1) % 2][:, 0:P * (t + 1)].rearrange("p (s q) -> p s q", q=P), ACT.Copy)\
                            .then_inc(sem("turned_out"), 1)
                    if 0 <= n - 2 < N and a.items[n - 2][1] == 1 and kind != "diff":
                        h, _ = a.items[n - 2]
                        act.wait_ge(sem("head_taken"), h0 + h + 1)
                        A(HHI[:, a.out + h, :], head_out(h), ACT.Copy).then_inc(sem("head_hi"), 1)

            def pool():
                def leave(m, bank):
                    act.wait_ge(sem("pool_mixed"), m + 1)
                    A(HHI[:, 8 + m, :], TM[:, m % 2, :], ACT.Copy).then_inc(sem("pool_hi"), 1)
                short(POOL_RUN, leave)

            def conv(l, o0):
                act.wait_ge(sem("lru_abs"), 1)
                A(small(SM + 8, 8), small(SM, 8), ACT.Exp, scale=-1.0).then_inc(sem("lru_exp"), 1)
                for n in range(8):
                    act.wait_ge(sem("conv_done"), n + 1)
                    A(BIGR[:, CD_XHI + n, :], M[:, n, :], ACT.Copy).then_inc(sem("conv_hi"), 1)
                    if n % 2:
                        yield

            def lru():
                def leave(m, bank):
                    name, dst = ("lru_ba", CD_GR) if m < 8 else ("lru_bx", CD_GI)
                    A(BIG[:, dst + m % 8, :], bank[:, 0:T], ACT.Sigmoid, bias=vcol(name, m % 8))\
                        .then_inc(sem("bank_free"), 1)
                short(LRU_RUN, leave)

            def states(l, o0):
                la = BIG[:, CD_GR:CD_GR + 8, :]
                act.wait_ge(sem("log_a"), 1)
                A(BIG[:, CD_XHI:CD_XHI + 8, :], la, ACT.Exp).then_inc(sem("lru_a"), 1)
                yield
                A(BIG[:, CD_XLO:CD_XLO + 8, :], la, ACT.Tanh).then_inc(sem("lru_a"), 1)
                for _ in range(4):
                    yield
                act.wait_ge(sem("lru_m2"), 1)
                A(la, la, ACT.Sqrt).then_inc(sem("lru_mult"), 1)

            def lru_out():
                y = BIG[:, CD_YG:CD_YG + 8, :]
                A(y, y, ACT.Gelu_apprx_tanh).then_inc(sem("lru_gelu"), 1)
                act.wait_ge(sem("lru_out"), 1)
                A(HHI[:, 8:16, :], M[:, 0:8, :], ACT.Copy).then_inc(sem("lru_hi"), 1)

            def mla_norm():
                square_sum(4, lambda k: big(CD_CQ + k))
                rstd(512)
                normed([BIGR[:, CD_NHI + k, :] for k in range(4)])
                square_sum(2, lambda k: big(CD_CKV + k))
                rstd(256)
                normed([BIGR[:, CD_NHI + 4 + k, :] for k in range(2)])

            def mla():
                copy_to = lambda at: lambda m, bank: A(big(at + m), bank[:, 0:T], ACT.Copy).then_inc(sem("bank_free"), 1)
                short(Q_RUN, copy_to(CD_QN))
                act.wait_ge(sem("angles"), 1)
                A(big(CD_SIN), TM[:, 6, :], ACT.Sin).then_inc(sem("sines"), 1)
                A(big(CD_COS), TM[:, 7, :], ACT.Sin).then_inc(sem("sines"), 1)
                short(KN_RUN, copy_to(CD_KN))
                short(KV_RUN, lambda m, bank: A(tokens(CD_V, 8)[:, m % 2, m // 2 * 2 * P:(m // 2 + 1) * 2 * P],
                                                bank[:, 0:T], ACT.Copy)
                      .then_inc(sem("bank_free"), 1))

            def log_gates(l, o0):
                act.wait_ge(sem("forget_abs"), l + 1)
                A(TM[32:36, 1, :], TM[32:36, 1, :], ACT.Exp, scale=-1.0).then_inc(sem("forget_exp"), 1)
                act.wait_ge(sem("forget_exp"), 2 * l + 1)
                A(TM[32:36, 1, :], TM[32:36, 1, :], ACT.Ln, bias=1.0).then_inc(sem("forget_exp"), 1)
                for _ in range(6):
                    yield
                act.wait_ge(sem("lam_summed"), l + 1)
                A(small(LAM_E, 2), BANK[6][:, 0:2], ACT.Exp).then_inc(sem("lam_exp"), 1)

            def head_norm(kind, l):
                n = step_no(c, "head_norm")
                A(M[:, 4:8, :], M[:, 0:4, :], ACT.Square).then_inc(sem("head_squared"), 1)
                if kind == "gla":
                    yield
                act.wait_ge(sem("head_mean"), n)
                A(M[:, 4:8, :], M[:, 4:8, :], ACT.Sqrt).then_inc(sem("head_root"), 1)
                if kind == "diff":
                    act.wait_ge(sem("head_gated"), l + 1)
                    A(HHI[:, 4:8, :], M[:, 0:4, :], ACT.Copy).then_inc(sem("heads_hi"), 1)

            def gla(l, o0):
                q = BIG[:, Z_GQ:Z_GQ + 2, :]
                act.wait_ge(sem("bank_free"), o0)
                A(q, q, ACT.Copy, scale=64 ** -0.5).then_inc(sem("gla_scaled"), 1)
                act.wait_ge(sem("decay_abs"), l + 1)
                A(TM[:, 6:8, :], TM[:, 6:8, :], ACT.Exp, scale=-1.0).then_inc(sem("decay_exp"), 1)
                act.wait_ge(sem("decay_exp"), 2 * l + 1)
                A(TM[:, 6:8, :], TM[:, 6:8, :], ACT.Ln, bias=1.0).then_inc(sem("decay_exp"), 1)
                yield
                for n, B in enumerate(LEVELS[:-1]):
                    act.wait_ge(sem("decays"), step_no(c, "decays"))
                    A(EXPS, EXPS, ACT.Exp).then_inc(sem("decays_exp"), 1)
                    yield
                for gate in range(4):
                    z = BIG[:, Z_G + 4 * gate:Z_G + 4 * gate + 4, :]
                    A(z, z, ACT.Silu).then_inc(sem("silu"), 1)
                    if gate % 2:
                        yield
                act.wait_ge(sem("gla_taken"), l + 1)
                yield from head_norm("gla", l)

            def take_gla():
                A(HHI[:, 12:16, :], BIG[:, Z_G + 12:Z_G + 16, :], ACT.Copy).then_inc(sem("gla_hi"), 1)

            def finish():
                rstd(D_MODEL)

            schedule(Engine(
                load_tables=load_tables, square_sum_x=lambda first=False: square_sum(KT, lambda k: X[:, k, :]),
                rstd=rstd, norm_in=lambda name, l: normed([HHI[:, k, :] for k in range(KT)]), run=run,
                meet=lambda: meet(act, "act", c), index=index, windows=lambda: None, attend=attend, pool=pool,
                post_norm=post_norm, conv=conv, lru=lru, states=states, mla_norm=mla_norm, lru_out=lru_out, mla=mla, rotate=lambda l: None,
                log_gates=log_gates, take_gla=take_gla, head_norm=lambda kind, l: whole(head_norm(kind, l)), gla=gla, finish=lambda: None))

        @block.vector
        def _(dve):
            c = {}
            v = nc.vector
            TT, TS, STT = v.tensor_tensor, v.tensor_scalar, v.scalar_tensor_tensor

            def then(ins):
                ins.then_inc(sem("dve_step"), 1)
                dve.wait_ge(sem("dve_step"), step_no(c, "dve_step"))

            def low(at, i, per):
                if isinstance(i, int) and i * per + at >= n_units:
                    return
                dve.wait_ge(sem("hi_done"), i * per + (at + 1))
                TT(WLO[at % SPLIT][:, :, :], RING[at % RAW][:, :].rearrange("p (k n) -> p k n", k=UB),
                   WHI[at % SPLIT][:, :, :].bitcast(f32), ALU.subtract).then_inc(sem("lo_done"), 1)

            def load_tables():
                for u in range(SPLIT):
                    low(u, 0, 0)
                dve.wait_ge(sem("tables"), 64)

            def run(r, beside=None, l=0):
                u0, o0 = begin(c, r.units, r.n)
                upo = r.blocks // UB
                per = BANKS * upo
                if r.kind == "ffn":
                    p0 = c.get("pairs", 0)
                    c["pairs"] = p0 + r.n // 2
                    f0 = 2 * p0

                def step(i, j):
                    bank = BANK[(o0 + j) % BANKS]
                    for h in range(upo - 1):
                        low(u0 + SPLIT + j * upo + h, i, per)
                    if r.kind in ("add", "ffn"):
                        dve.wait_ge(sem("unit_used"), i * per + (u0 + (j + 1) * upo))
                    if r.kind == "add":
                        x = X[:, i * BANKS + j, :]
                        TT(x, x, bank[:, 0:T], ALU.add).then_inc(sem("bank_free"), 1)
                    if r.kind == "ffn":
                        if j % 2 == 0 and least(i) * 2 + p0 + j // 2 >= 2:
                            dve.wait_ge(sem("gated"), i * 2 + (p0 + j // 2 - 1))
                        z, wc = TM[:, j, :], lambda k: vcol("ffn_w", i * BANKS + (192 * r.dst + 64 * k + j))
                        TS(z, bank[:, 0:T], wc(2), vcol("ffn_b", i * BANKS + (64 * r.dst + j)), ALU.mult, ALU.add)\
                            .then_inc(sem("conv"), 1)
                        dve.wait_ge(sem("conv"), i * (2 * BANKS) + (2 * (f0 + j) + 1))
                        STT(z[:, 1:T], bank[:, 0:T - 1], wc(1), z[:, 1:T], ALU.mult, ALU.add).then_inc(sem("conv"), 1)
                        dve.wait_ge(sem("conv"), i * (2 * BANKS) + (2 * (f0 + j) + 2))
                        STT(z[:, 2:T], bank[:, 0:T - 2], wc(0), z[:, 2:T], ALU.mult, ALU.add)\
                            .then_inc(sem("bank_free"), 1)
                    low(u0 + SPLIT + j * upo + upo - 1, i, per)

                groups(dve, r, step, beside and beside(l, o0))

            def short(r, leave=None):
                u0, o0 = begin(c, r.n * r.blocks // UB, r.n)
                for m in range(r.n):
                    if leave:
                        dve.wait_ge(sem("short_out"), c.get("short_out", 0) + m + 1)
                        leave(m, BANK[(o0 + m) % BANKS])
                    if r.ends_unit(m):
                        low(u0 + SPLIT + ((m + 1) * r.blocks // UB - 1), 0, 0)
                c["short_out"] = c.get("short_out", 0) + r.n

            def rstd(width, sums=None):
                n = step_no(c, "rstd")
                dve.wait_ge(sem("summed"), c["summed"])
                TS(TM[:, 10, :], BANK[7][:, 0:T], 1.0 / width, EPS, ALU.mult, ALU.add).then_inc(sem("mean_sq"), 1)
                dve.wait_ge(sem("root"), n)
                then(v.reciprocal(TM[:, 10, :], TM[:, 11, :]))

            c["summed"] = 0

            def squares(n):
                c["summed"] += n

            def normed(src, gain, hi, lo):
                n = len(hi)
                g0 = c.get("normed", 0)
                c["normed"] = g0 + n
                for k in range(n + 1):
                    if k < n:
                        STT(TM[:, 4 + k % 4, :], src(k), gain(k), TM[:, 10, :], ALU.mult, ALU.mult).then_inc(sem("normed"), 1)
                    if k:
                        dve.wait_ge(sem("normed_hi"), g0 + k)
                        TT(lo[k - 1], TM[:, 4 + (k - 1) % 4, :], hi[k - 1].bitcast(f32), ALU.subtract)\
                            .then_inc(sem("normed_lo"), 1)

            def norm_in(name, l):
                normed(lambda k: X[:, k, :], lambda k: vcol(name, KT * l + k),
                       [HHI[:, k, :] for k in range(KT)], [HLO[:, k, :] for k in range(KT)])

            def post_norm(name, l):
                squares(1)
                rstd(D_MODEL)
                for k in range(KT):
                    then(STT(TM[:, 8 + k % 2, :], M[:, k, :], vcol(name, KT * l + k), TM[:, 10, :], ALU.mult, ALU.mult))
                    TT(X[:, k, :], X[:, k, :], TM[:, 8 + k % 2, :], ALU.add).then_inc(sem("x_new"), 1)
                squares(KT)

            def index(l, o0):
                dve.wait_ge(sem("bank_free"), o0)
                k = BIG[:, AB_MISC, :]
                v.memset(BIG[64:128, AB_KI, :], 0.0)
                v.memset(BIG[0:64, AB_KI + 1, :], 0.0)
                v.tensor_copy(BIG[0:64, AB_KI, :], k[0:64])
                v.tensor_copy(BIG[64:128, AB_KI + 1, :], k[64:128]).then_inc(sem("keys_padded"), 1)
                for n in range(32):
                    t, h = divmod(n, 16)
                    W = P * (t + 1)
                    wi = tokens(AB_WI, 2)[:, t, h:h + 1]
                    dve.wait_ge(sem("rectified"), n + 1)
                    if n:
                        dve.wait_ge(sem("weighed"), n)
                    if h == 0:
                        TS(big(AB_ACC + t, 0, W), TM[:, n % 4, 0:W], wi, None, ALU.mult).then_inc(sem("weighed"), 1)
                    else:
                        STT(big(AB_ACC + t, 0, W), TM[:, n % 4, 0:W], wi, big(AB_ACC + t, 0, W), ALU.mult, ALU.add)\
                            .then_inc(sem("weighed"), 1)
                    if n % 4 == 3:
                        yield
                dve.wait_ge(sem("weighed"), 32)
                work = [TM[:, 4 + t, 0:P * (t + 1)] for t in (0, 1)]
                mask = table_mask("chunk")
                TT(work[0], big(AB_ACC, 0, P), mask(0, 0), ALU.add)
                then(TT(work[1], big(AB_ACC + 1), mask(0, 1), ALU.add))
                for _ in range(K_TOP // 8):
                    v.max(small(TOP8, 8), work[0])
                    then(v.max(small(SM, 8), work[1]))
                    v.match_replace(work[0], small(TOP8, 8), work[0], TAKEN)
                    then(v.match_replace(work[1], small(SM, 8), work[1], TAKEN))
                    yield
                for t in (0, 1):
                    TS(big(AB_SEL + t, 0, P * (t + 1)), work[t], TAKEN, NEG, ALU.not_equal, ALU.mult)\
                        .then_inc(sem("selected"), 1)
                dve.wait_ge(sem("selected"), 2)

            def attend(kind, l=0):
                a = Attention(kind)
                g0, h0 = c.get("item", 0), c.get("head", 0)
                N = len(a.items)
                c["item"], c["head"] = g0 + N, h0 + a.heads
                hi0 = c.get("head_hi", 0)
                c["head_hi"] = hi0 + (a.heads if kind != "diff" else 0)
                for n in range(N + 4):
                    if n < N:
                        h, t = a.items[n]
                        W = P * (t + 1)
                        dve.wait_ge(sem("scored"), g0 + n + 1)
                        if g0 + n >= 2:
                            dve.wait_ge(sem("turned"), g0 + n - 1)
                        for j in range(a.sets):
                            last = STT(score(n, j, W), BANK[4 + 2 * (n % 2) + j][:, 0:W], a.scale, a.mask(h, t),
                                       ALU.mult, ALU.add)
                        last.then_inc(sem("masked"), 1)
                        dve.wait_ge(sem("masked"), g0 + n + 1)
                        for j in range(a.sets):
                            last = v.tensor_reduce(small(NEG_MAX + 2 * (n % 2) + j), score(n, j, W), AX.X, ALU.max,
                                                   negate=True)
                        last.then_inc(sem("maxed"), 1)
                    if 0 <= n - 1 < N:
                        h, t = a.items[n - 1]
                        W, k = P * (t + 1), 2 * ((n - 1) % 2)
                        dve.wait_ge(sem("powered"), g0 + n)
                        then(v.reciprocal(small(RECIPS + k, a.sets), small(SUMS + k, a.sets)))
                        first = TS(score(n - 1, 0, W), score(n - 1, 0, W), small(RECIPS + k), None, ALU.mult)
                        if a.sets == 1:
                            first.then_inc(sem("normalised"), 1)
                        else:
                            then(TT(small(RECIPS + k + 1), small(RECIPS + k + 1), small(NEG_LAM), ALU.mult))
                            STT(score(n - 1, 0, W), score(n - 1, 1, W), small(RECIPS + k + 1), score(n - 1, 0, W),
                                ALU.mult, ALU.add).then_inc(sem("normalised"), 1)
                    if 0 <= n - 2 < N and a.items[n - 2][1] == 1:
                        h, _ = a.items[n - 2]
                        dve.wait_ge(sem("head_done"), h0 + h + 1)
                        dst = M[:, h, :] if kind == "diff" else head_out(h)
                        if a.gated:
                            TT(dst, BANK[h % 2][:, 0:T], big(Z_G + a.out + h), ALU.mult).then_inc(sem("head_taken"), 1)
                        else:
                            v.tensor_copy(dst, BANK[h % 2][:, 0:T]).then_inc(sem("head_taken"), 1)
                    if 0 <= n - 3 < N and a.items[n - 3][1] == 1 and kind != "diff":
                        h, _ = a.items[n - 3]
                        dve.wait_ge(sem("head_hi"), hi0 + h + 1)
                        TT(HLO[:, a.out + h, :], head_out(h), HHI[:, a.out + h, :].bitcast(f32), ALU.subtract)

            def pool():
                def leave(m, bank):
                    if m >= 2:
                        dve.wait_ge(sem("pool_hi"), m - 1)
                    TS(TM[:, m % 2, :], bank[:, 0:T], vcol("pool_b", m), vcol("pool_scale", m), ALU.add, ALU.mult)\
                        .then_inc(sem("pool_mixed"), 1)
                    dve.wait_ge(sem("pool_hi"), m + 1)
                    TT(HLO[:, 8 + m, :], TM[:, m % 2, :], HHI[:, 8 + m, :].bitcast(f32), ALU.subtract)\
                        .then_inc(sem("bank_free"), 1)
                short(POOL_RUN, leave)

            def conv(l, o0):
                dve.wait_ge(sem("bank_free"), o0)
                lam = V[:, VO["lru_lam"]:VO["lru_lam"] + 8]
                STT(small(SM, 8), lam, -1.0, lam, ALU.mult, ALU.max).then_inc(sem("lru_abs"), 1)
                wc = lambda k, n: vcol("lru_w", 8 * k + n)
                for n in range(0, 8, 2):
                    pair = [(m, big(CD_XL + m), M[:, m, :]) for m in (n, n + 1)]
                    then([TS(y, x, wc(3, m), vcol("lru_b", m), ALU.mult, ALU.add) for m, x, y in pair][1])
                    for d in (1, 2):
                        then([STT(y[:, d:T], x[:, 0:T - d], wc(3 - d, m), y[:, d:T], ALU.mult, ALU.add)
                              for m, x, y in pair][1])
                    for m, x, y in pair:
                        STT(y[:, 3:T], x[:, 0:T - 3], wc(0, m), y[:, 3:T], ALU.mult, ALU.add).then_inc(sem("conv_done"), 1)
                    for m in (n, n + 1):
                        dve.wait_ge(sem("conv_hi"), m + 1)
                        TT(BIGR[:, CD_XLO + m, :], M[:, m, :], BIGR[:, CD_XHI + m, :].bitcast(f32), ALU.subtract)\
                            .then_inc(sem("conv_split"), 1)
                    yield
                dve.wait_ge(sem("lru_exp"), 1)
                e, z, z2, p = small(SM + 8, 8), small(SM, 8), small(SM + 16, 8), small(LRU_C, 8)
                then(TS(z, e, 2.0, None, ALU.add))
                then(v.reciprocal(z, z))
                then(TT(z, z, e, ALU.mult))
                then(TT(z2, z, z, ALU.mult))
                then(TS(p, z2, 1.0 / 19, None, ALU.mult))
                for d in range(17, 2, -2):
                    then(STT(p, p, 1.0 / d, z2, ALU.add, ALU.mult))
                yield
                then(STT(p, p, 1.0, z, ALU.add, ALU.mult))
                then(TS(e, lam, -1.0, 0.0, ALU.mult, ALU.max))
                then(STT(p, p, 2.0, e, ALU.mult, ALU.add))
                then(TS(p, p, -8.0, None, ALU.mult))

            def states(l, o0):
                dve.wait_ge(sem("bank_free"), o0)
                for n in range(8):
                    last = TS(big(CD_GR + n), big(CD_GR + n), small(LRU_C + n), None, ALU.mult)
                last.then_inc(sem("log_a"), 1)
                yield
                r, i, th = (BIG[:, at:at + 8, :] for at in (CD_GR, CD_GI, CD_XLO))
                then(TT(i, i, M[:, 0:8, :], ALU.mult))
                yield
                dve.wait_ge(sem("lru_a"), 2)
                den = M[:, 8:16, :]
                then(TS(den, th, -1.0, 1.0, ALU.mult, ALU.add))
                yield
                then(v.reciprocal(den, den))
                yield
                then(TS(th, th, -2.0, None, ALU.mult))
                TT(r, th, den, ALU.mult).then_inc(sem("lru_m2"), 1)
                yield
                yield
                dve.wait_ge(sem("lru_mult"), 1)
                then(TT(i, i, r, ALU.mult))
                yield
                for n in range(8):
                    last = v.tensor_tensor_scan(M[:, n, :], big(CD_XHI + n), big(CD_GI + n), 0.0, ALU.mult, ALU.add)
                then(last)

            def lru_out():
                dve.wait_ge(sem("lru_gelu"), 1)
                TT(M[:, 0:8, :], M[:, 0:8, :], BIG[:, CD_YG:CD_YG + 8, :], ALU.mult).then_inc(sem("lru_out"), 1)
                dve.wait_ge(sem("lru_hi"), 1)
                TT(HLO[:, 8:16, :], M[:, 0:8, :], HHI[:, 8:16, :].bitcast(f32), ALU.subtract)

            def rope(tiles):
                for n, (k, rot, cos, sin) in enumerate(tiles):
                    g = step_no(c, "rope")
                    dve.wait_ge(sem("rope_done"), g)
                    TT(TM[:, 2 + n % 2, :], BANK[4 + n % 2][:, 0:T], sin, ALU.mult).then_inc(sem("rope_read"), 1)
                    then(TT(big(k), big(k), cos, ALU.mult))
                    last = TT(big(k), big(k), TM[:, 2 + n % 2, :], ALU.add)
                    yield
                then(last)

            def mla_norm():
                squares(4)
                rstd(512)
                bigr = lambda at, n: [BIGR[:, at + k, :] for k in range(n)]
                normed(lambda k: big(CD_CQ + k), lambda k: vcol("q_norm", k), bigr(CD_NHI, 4), bigr(CD_NLO, 4))
                squares(2)
                rstd(256)
                normed(lambda k: big(CD_CKV + k), lambda k: vcol("kv_norm", k), bigr(CD_NHI + 4, 2), bigr(CD_NLO + 4, 2))

            def mla():
                then(v.tensor_copy(TM[:, 4, :], POS[:, :]))
                ang = TM[:, 5, :]
                then(TS(ang, TM[:, 4, :], tcol("freq", 1), None, ALU.mult))
                magic = 1.5 * 2.0 ** 23
                for k, (r, turn) in enumerate(((TM[:, 6, :], 0.0), (TM[:, 7, :], 0.25))):
                    q = TM[:, 8, :]
                    then(TS(q, ang, 1 / (2 * np.pi), turn, ALU.mult, ALU.add))
                    then(TS(q, q, magic, None, ALU.add))
                    then(TS(q, q, -magic, None, ALU.add))
                    then(STT(r, q, -6.28125, ang, ALU.mult, ALU.add))
                    then(STT(r, q, -1.9350051879882812e-3, r, ALU.mult, ALU.add))
                    then(STT(r, q, -3.0199159819567529e-7, r, ALU.mult, ALU.add))
                    then(TS(r, r, 2 * np.pi * turn, None, ALU.add))
                    last = TS(r, r, 3.1415925, -3.1415925, ALU.min, ALU.max)
                last.then_inc(sem("angles"), 1)
                short(Q_RUN)
                short(KN_RUN)
                short(KV_RUN)
                dve.wait_ge(sem("sines"), 2)
                dve.wait_ge(sem("bank_free"), c["output"])
                whole(rope(MLA_ROPE))
                v.memset(BIG[64:128, CD_KRZ, :], 0.0)
                v.memset(BIG[0:64, CD_KRZ + 1, :], 0.0)
                v.tensor_copy(BIG[0:64, CD_KRZ, :], BIG[0:64, CD_KR, :])
                v.tensor_copy(BIG[64:128, CD_KRZ + 1, :], BIG[64:128, CD_KR, :]).then_inc(sem("rope_keys"), 1)
                dve.wait_ge(sem("rope_keys"), 1)

            def decay_sums(l):
                dve.wait_ge(sem("decay_logit"), l + 1)
                for i in (0, 1):
                    last = TS(TM[:, 4 + i, :], BANK[5][:, i * T:(i + 1) * T], vcol("gla_ba", 2 * l + i), None, ALU.add)
                then(last)
                STT(TM[:, 6:8, :], TM[:, 4:6, :], -1.0, TM[:, 4:6, :], ALU.mult, ALU.max).then_inc(sem("decay_abs"), 1)
                dve.wait_ge(sem("decay_exp"), 2 * l + 2)
                then(STT(TM[:, 4:6, :], TM[:, 4:6, :], 0.0, TM[:, 6:8, :], ALU.min, ALU.subtract))
                then(TS(TM[:, 4:6, :], TM[:, 4:6, :], 1.0 / 16, None, ALU.mult))
                for i in (0, 1):
                    last = v.tensor_tensor_scan(CUM[:, i, :], tcol("ones", T), TM[:, 4 + i, :], 0.0, ALU.mult, ALU.add)
                then(last)

            def log_gates(l, o0):
                rows = slice(32, 36)
                x, e = TM[rows, 0, :], TM[rows, 1, :]
                dve.wait_ge(sem("bank_free"), o0)
                turn = rope(ROPE_DIFF)
                then(TS(x, BIG[rows, Z_MISC, :], V[rows, VO["fox_fb"] + l:VO["fox_fb"] + l + 1], None, ALU.add))
                STT(e, x, -1.0, x, ALU.mult, ALU.max).then_inc(sem("forget_abs"), 1)
                next(turn)
                dve.wait_ge(sem("forget_exp"), 2 * l + 2)
                then(STT(x, x, 0.0, e, ALU.min, ALU.subtract))
                v.tensor_tensor_scan(e, TB[rows, TO["ones"]:TO["ones"] + T], x, 0.0, ALU.mult, ALU.add)\
                    .then_inc(sem("forget_sum"), 1)
                yield
                next(turn)
                dve.wait_ge(sem("forget_cols"), l + 1)
                v.tensor_copy(small(FOX_F, 8), BANK[6][:, 0:8]).then_inc(sem("forget_taken"), 1)
                dve.wait_ge(sem("forget_taken"), l + 1)
                lf = V[0:64, VO["diff_lam"] + 4 * l:VO["diff_lam"] + 4 * l + 4].rearrange("p (a b) -> p a b", b=2)
                TT(SMALL[0:64, LAM_E:LAM_E + 2], lf[:, :, 0], lf[:, :, 1], ALU.mult).then_inc(sem("lam_products"), 1)
                yield
                for h in range(4):
                    next(turn)
                    dve.wait_ge(sem("forget_rows"), 4 * l + h + 1)
                    for t in (0, 1):
                        W = P * (t + 1)
                        last = STT(M[:, 2 * h + t, 0:W], BANK[7 - h % 2][:, 0:W], small(FOX_F + 4 * t + h),
                                   table_mask("causal")(h, t), ALU.subtract, ALU.subtract, reverse1=True)
                    last.then_inc(sem("fox_bias"), 1)
                    yield
                next(turn)
                dve.wait_ge(sem("lam_exp"), l + 1)
                then(TT(small(NEG_LAM), small(LAM_E + 1), small(LAM_E), ALU.subtract))
                then(TS(small(NEG_LAM), small(NEG_LAM), -LAM0[l], None, ALU.add))
                yield
                whole(turn)

            LAM0 = [0.8 - 0.6 * float(np.exp(-0.3 * l)) for l in (0, 1)]

            def take_gla():
                n = step_no(c, "gla_hi")
                dve.wait_ge(sem("gla_hi"), n)
                TT(HLO[:, 12:16, :], BIG[:, Z_G + 12:Z_G + 16, :], HHI[:, 12:16, :].bitcast(f32), ALU.subtract)

            def head_norm(kind, l):
                n = step_no(c, "head_norm")
                dve.wait_ge(sem("head_summed"), n)
                for half in (0, 1):
                    last = TS(M[:, 4 + 2 * half:6 + 2 * half, :].rearrange("p a b -> p (a b)"), BANK[5 + half][:, :],
                              1.0 / P, EPS, ALU.mult, ALU.add)
                last.then_inc(sem("head_mean"), 1)
                dve.wait_ge(sem("head_root"), n)
                then(v.reciprocal(M[:, 4:8, :], M[:, 4:8, :]))
                then(STT(M[:, 0:4, :], M[:, 0:4, :], vcol(f"{kind}_norm", l), M[:, 4:8, :], ALU.mult, ALU.mult))
                at = 4 if kind == "diff" else 12
                gate = BIG[:, Z_G + at:Z_G + at + 4, :]
                if kind == "gla":
                    dve.wait_ge(sem("silu"), 4 * (l + 1))
                    TT(gate, M[:, 0:4, :], gate, ALU.mult)
                    return
                STT(M[:, 0:4, :], M[:, 0:4, :], 1.0 - LAM0[l], gate, ALU.mult, ALU.mult).then_inc(sem("head_gated"), 1)
                dve.wait_ge(sem("heads_hi"), l + 1)
                TT(HLO[:, 4:8, :], M[:, 0:4, :], HHI[:, 4:8, :].bitcast(f32), ALU.subtract)

            def gla(l, o0):
                dve.wait_ge(sem("bank_free"), o0)
                decay_sums(l)
                yield
                q, k = BIG[:, Z_GQ:Z_GQ + 2, :], BIG[:, Z_GK:Z_GK + 2, :]
                dve.wait_ge(sem("gla_scaled"), l + 1)
                dve.wait_ge(sem("gla_zeroed"), l + 1)
                masks = tcol("gla_mask", 192).rearrange("p (l t) -> p l t", l=6)
                n0 = 9 * l
                for n, B in enumerate(LEVELS):
                    if B:
                        e = EXPS.rearrange("p (a i m r) -> p a i m r", a=2, i=2, r=B)
                        even, odd = blocks(CUM, 0, B), blocks(CUM, 1, B)
                        ref = even[:, :, :, B - 1:B].broadcast_to([P, 2, P // B, B])
                        TT(e[:, 0], odd, ref, ALU.subtract)
                        TT(e[:, 1], ref, even, ALU.subtract).then_inc(sem("decays"), 1)
                        dve.wait_ge(sem("decays_exp"), 8 * l + n + 1)
                    if n:
                        dve.wait_ge(sem("level_scored"), n0 + n)
                    if B:
                        TT(blocks(QQ, 1, B), blocks(q, 1, B), e[:, 0], ALU.mult)
                        for par in (0, 1):
                            half = slice(64 * par, 64 * par + 64)
                            last = TT(blocks(KK[half, par], 0, B), blocks(k[half], 0, B), e[half, 1], ALU.mult)
                    else:
                        v.tensor_copy(QQ, q)
                        for par in (0, 1):
                            half = slice(64 * par, 64 * par + 64)
                            last = v.tensor_copy(KK[half, par], k[half])
                    last.then_inc(sem("level_ready"), 1)
                    yield
                    dve.wait_ge(sem("level_scored"), n0 + n + 1)
                    if B == 128:
                        then(v.tensor_copy(ST[:, :, 0, P:T], BANK[4][:, :].rearrange("p (h t) -> p h t", h=4)))
                    elif B == 64:
                        sc = BANK[5][0:64, :].rearrange("p (h m t) -> p h m t", h=4, m=2)
                        for m in (0, 1):
                            last = v.tensor_copy(ST[0:64, :, m, m * P + 64:m * P + P], sc[:, :, m, :])
                        then(last)
                    elif B == 32:
                        sc = BANK[6][:, 0:256].rearrange("p (h m t) -> p h m t", h=4, m=2)
                        for m in range(4):
                            r = 64 * (m % 2)
                            last = v.tensor_copy(ST[r:r + 32, :, m // 2, 64 * m + 32:64 * m + 64], sc[r:r + 32, :, m // 2, :])
                        then(last)
                    else:
                        mask = masks[:, n - 3:n - 2, :].broadcast_to([P, 8, 32])
                        sc = BANK[7][:, 0:256].rearrange("p (a t) -> p a t", a=8)
                        to = DIAG if n == 3 else DIAG_NEW
                        then(TT(to.rearrange("p (a t) -> p a t", a=8), sc, mask, ALU.mult))
                        if n > 3:
                            then(TT(DIAG, DIAG, DIAG_NEW, ALU.add))
                d = DIAG.rearrange("p (h s t) -> p h s t", h=4, s=2)
                for j in range(8):
                    r, s = 32 * (j % 4), j // 4
                    last = v.tensor_copy(ST[r:r + 32, :, s, 32 * j:32 * j + 32], d[r:r + 32, :, s, :])
                last.then_inc(sem("gla_scores"), 1)
                yield
                dve.wait_ge(sem("gla_out"), 4 * l + 4)
                for h in range(4):
                    last = v.tensor_copy(M[:, h, :], BANK[4 + h % 2][:, (h // 2) * T:(h // 2 + 1) * T])
                last.then_inc(sem("gla_taken"), 1)
                yield
                head_norm("gla", l)

            def finish():
                for k in range(KT):
                    STT(M[:, k, :], X[:, k, :], vcol("final", k), TM[:, 10, :], ALU.mult, ALU.mult)\
                        .then_inc(sem("final"), 1)

            schedule(Engine(
                load_tables=load_tables, square_sum_x=lambda first=False: squares(KT), rstd=rstd, norm_in=norm_in,
                run=run, meet=lambda: meet(dve, "dve", c), index=index, windows=lambda: None, attend=attend,
                pool=pool, post_norm=post_norm, conv=conv, lru=lambda: short(LRU_RUN), states=states,
                mla_norm=mla_norm, lru_out=lru_out, mla=mla,
                rotate=lambda l: whole(rope(ROPE_MOBA)), log_gates=log_gates, take_gla=take_gla, head_norm=head_norm, gla=gla,
                finish=finish))

        @block.gpsimd
        def _(pool):
            c = {}
            g = nc.gpsimd

            def then(ins):
                ins.then_inc(sem("pool_step"), 1)
                pool.wait_ge(sem("pool_step"), step_no(c, "pool_step"))

            def run(r, beside=None, l=0):
                if beside:
                    beside(l)
                if r.kind == "m":
                    g0 = c.get("m_outputs", 0)
                    c["m_outputs"] = g0 + r.n

                    def step(i, j):
                        pool.wait_ge(sem("sq_done"), i * BANKS + (g0 + j + 1))
                        if isinstance(i, int) and i == 0 and j == 0:
                            g.tensor_copy(TM[:, 4, :], TM[:, 0, :]).then_inc(sem("sq_added"), 1)
                        else:
                            pool.wait_ge(sem("sq_added"), i * BANKS + (g0 + j))
                            g.tensor_tensor(TM[:, 4, :], TM[:, 4, :], TM[:, j, :], ALU.add).then_inc(sem("sq_added"), 1)
                    groups(pool, r, step)
                if r.kind == "ffn":
                    p0 = c.get("pairs", 0)
                    c["pairs"] = p0 + r.n // 2

                    def step(i, j):
                        if j % 2 == 0:
                            return
                        k = j // 2
                        done = i * 2 + (p0 + k + 1)
                        pool.wait_ge(sem("gelu_done"), done)
                        a = TM[:, 6 + k, :]
                        g.tensor_tensor(a, TM[:, 4 + k, :], TM[:, j, :], ALU.mult).then_inc(sem("gated"), 1)
                        pool.wait_ge(sem("gated"), done)
                        g.tensor_copy(BIGR[:, i * 2 + k, :], a).then_inc(sem("hid_hi"), 1)
                        pool.wait_ge(sem("hid_hi"), done)
                        g.tensor_tensor(BIGR[:, i * 2 + (FF_T + k), :], a, BIGR[:, i * 2 + k, :].bitcast(f32), ALU.subtract)\
                            .then_inc(sem("hid_lo"), 1)
                    groups(pool, r, step)

            def windows():
                pool.wait_ge(sem("bank_free"), RUNS_INDEX[0].n + RUNS_INDEX[1].n + RUN_QKU.n)
                for gr in range(4):
                    u = BIG[:, AB_U + 2 * gr:AB_U + 2 * gr + 2, :]
                    src = u
                    for lev in range(gr + 1):
                        d = 1 << lev
                        dst = M[:, 2 * (lev % 2):2 * (lev % 2) + 2, :]
                        g.tensor_copy(dst[:, :, 0:d], src[:, :, 0:d])
                        then(g.tensor_tensor(dst[:, :, d:T], src[:, :, d:T], src[:, :, 0:T - d], ALU.add))
                        src = dst
                    mean = M[:, 4:6, :]
                    then(g.tensor_scalar(mean, src, 1.0 / (2 << gr), None, ALU.mult))
                    for k in (0, 1):
                        last = g.tensor_tensor(mean[:, k, 0:16], src[:, k, 0:16], tcol("pool_inv", 16, 16 * gr), ALU.mult)
                    then(last)
                    then(g.tensor_tensor(mean, mean, u, ALU.subtract))
                    hi = BIGR[:, AB_POOL + 2 * gr:AB_POOL + 2 * gr + 2, :]
                    lo = BIGR[:, AB_POOL + 8 + 2 * gr:AB_POOL + 10 + 2 * gr, :]
                    then(g.tensor_copy(hi, mean))
                    last = g.tensor_tensor(lo, mean, hi.bitcast(f32), ALU.subtract)
                last.then_inc(sem("pooled"), 1)

            def attend(kind, l=0):
                if kind == "diff":
                    k = BIG[:, Z_DK:Z_DK + 4, :]
                    g.memset(M[64:128, 8:12, :], 0.0)
                    g.memset(M[0:64, 12:16, :], 0.0)
                    g.tensor_copy(M[0:64, 8:12, :], k[0:64])
                    g.tensor_copy(M[64:128, 12:16, :], k[64:128]).then_inc(sem("keys_halved"), 1)

            def gla(l):
                pool.wait_ge(sem("decay_logit"), l + 1)
                g.memset(ST, 0.0)
                g.memset(QQ, 0.0)
                g.memset(KK, 0.0).then_inc(sem("gla_zeroed"), 1)

            nothing = lambda *a, **k: None
            schedule(Engine(
                load_tables=lambda: pool.wait_ge(sem("tables"), 64), square_sum_x=nothing, rstd=nothing,
                norm_in=nothing, run=run, meet=lambda: meet(pool, "pool", c), index=nothing, windows=windows,
                attend=attend, pool=nothing, post_norm=nothing, conv=nothing, lru=nothing, states=nothing,
                mla_norm=nothing, lru_out=nothing, mla=nothing,
                rotate=nothing, log_gates=nothing, take_gla=nothing, head_norm=nothing, gla=gla,
                finish=nothing))


def columns(a):
    return np.ascontiguousarray(a.reshape(-1, P).T)


def stream(a):
    K, N = a.shape
    b = a.reshape(K // P, P, N // P, P).transpose(2, 0, 1, 3).reshape(-1, UB, P, P)
    return b.transpose(0, 2, 1, 3).reshape(-1, P, UB * P)


def stream_pairs(a):
    K, N = a.shape
    return a.reshape(K // P, P, N // (2 * P), 2, P).transpose(2, 0, 3, 1, 4).reshape(-1, UB, P, P)\
        .transpose(0, 2, 1, 3).reshape(-1, P, UB * P)


def turn(half, dim):
    r = np.zeros((P, P), np.float32)
    for at in range(0, P, dim):
        for i in range(half):
            r[at + half + i, at + i] = -1.0
            r[at + i, at + half + i] = 1.0
    return r


def rope_tables(dim, rot, theta):
    freq = (theta ** (-np.arange(0, rot, 2) / rot)).astype(np.float32)
    ang = (np.arange(T, dtype=np.float32)[:, None] * freq[None, :]).astype(np.float32)
    cos, sin = np.ones((P, T), np.float32), np.zeros((P, T), np.float32)
    for at in range(0, P, dim):
        for half in (0, 1):
            rows = slice(at + half * rot // 2, at + (half + 1) * rot // 2)
            cos[rows], sin[rows] = np.cos(ang).T, np.sin(ang).T
    return cos, sin


def tables():
    t = {}
    t["ident"] = np.eye(P, dtype=np.float32)
    t["ones"] = np.ones((P, T), np.float32)
    q, k = np.arange(P)[:, None], np.arange(P)[None, :]
    off = np.zeros((P, P), np.float32)
    t["chunk"] = np.concatenate([off, np.where(k < (q // 64 + 1) * 64, 0, NEG)], 1)
    t["causal"] = np.concatenate([off, np.where(k <= q, 0, NEG)], 1)
    t["diff_cos"], t["diff_sin"] = rope_tables(64, 16, 500000.0)
    t["moba_cos"], t["moba_sin"] = rope_tables(128, 32, 500000.0)
    t["diff_rot"], t["moba_rot"], t["mla_rot"] = turn(8, 64), turn(16, 128), turn(32, 64)
    t["freq"] = (10000.0 ** (-(np.arange(P) % 32) / 32.0))[:, None]
    inv = np.stack([1.0 / np.minimum(np.arange(16) + 1, wn) for wn in (2, 4, 8, 16)])
    t["pool_inv"] = np.broadcast_to(inv.reshape(1, 64), (P, 64))
    s, tt = np.arange(P)[:, None] % 32, np.arange(32)[None, :]
    t["gla_mask"] = np.concatenate([((tt // B) % 2 == 1) & (s // B == tt // B - 1) for B in (16, 8, 4, 2, 1)]
                                   + [s == tt], 1)
    rows = np.zeros((P, 4, P), np.float32)
    for h in range(4):
        rows[32 + h, h, :] = 1.0
    t["head_row"] = rows.reshape(P, 512)
    return np.concatenate([np.asarray(t[n], np.float32) for n, _ in TAB], 1)


def parameters(i):
    def rows(a, at=0):
        o = np.zeros((P, a.shape[1]), a.dtype)
        o[at:at + a.shape[0]] = a
        return o
    v = {}
    for name, key in (("mix_pre", "mix_pre_g"), ("mix_post", "mix_post_g"), ("ffn_pre", "ffn_pre_g"),
                      ("ffn_post", "ffn_post_g"), ("norm2", "norm_g_2"), ("final", "final_norm_g_2"),
                      ("q_norm", "q_norm_g"), ("kv_norm", "kv_norm_g"), ("pool_b", "pool_b"),
                      ("pool_scale", "pool_scale"), ("lru_w", "lru_conv_w"), ("lru_b", "lru_conv_b"),
                      ("lru_ba", "lru_ba"), ("lru_bx", "lru_bx"), ("lru_lam", "lru_lambda"),
                      ("diff_norm", "diff_norm_g_2"), ("gla_norm", "gla_norm_g_2"), ("gla_ba", "gla_ba_2")):
        v[name] = columns(i[key])
    pairs = lambda a: a.reshape(-1, 2, FF_T, P).transpose(3, 0, 2, 1).reshape(P, -1)
    v["ffn_w"], v["ffn_b"] = pairs(i["ffn_conv_w"]), pairs(i["ffn_conv_b"])
    v["fox_fb"] = rows(i["fox_fb_2"].T, 32)
    v["diff_lam"] = rows(i["diff_lam_2"].reshape(8, 64).T)
    v["gla_wa2"] = rows(i["gla_wa2_2"].transpose(1, 0, 2).reshape(16, 512))
    return np.concatenate([v[n] for n, _ in VEC], 1)


def weights(i):
    parts = []
    pad = lambda a, n: np.concatenate([a, np.zeros((a.shape[0], n - a.shape[1]), a.dtype)], 1)
    q, k, v, qi, ki, wi, u = np.split(i["ab_w_in"][0], np.cumsum([1024, 1024, 1024, 1024, 64, 16]), 1)
    parts += [stream(a) for a in (qi, np.concatenate([ki, ki], 1))] + [stream_pairs(pad(wi, 2 * P))]
    parts += [stream(a) for a in (q, k, u)] + [stream_pairs(v)]
    parts += [np.concatenate([a.reshape(2, P, 2, P).transpose(2, 0, 1, 3).reshape(4, P, P) for a in i["pool_w"][0]])
              .reshape(2, UB, P, P).transpose(0, 2, 1, 3).reshape(2, P, UB * P)]

    def ffn(l):
        up = i["ffn_up"][l].reshape(D_MODEL, 2, FF_T, P).transpose(0, 2, 1, 3).reshape(D_MODEL, 2 * FF_T * P)
        return [stream(up), stream(i["ffn_down"][l])]
    parts += [stream(i["ab_w_out"][0])] + ffn(0)
    cq, ckv, kr, x, y = np.split(i["cd_w_in"][0], np.cumsum([512, 256, 64, 1024]), 1)
    parts += [stream(a) for a in (x, cq, ckv, np.concatenate([kr, kr], 1))]
    parts += [i[n][0].transpose(1, 0, 2).reshape(1, P, UB * P) for n in ("lru_wa", "lru_wx")] + [stream(y)]
    up = i["w_q_up"][0].reshape(512, 8, 192)
    parts += [stream(np.concatenate([up[:, :, :P].reshape(512, 1024), up[:, :, P:].reshape(512, 512)], 1))]
    up = i["w_kv_up"][0].reshape(256, 8, 256)
    parts += [stream(up[:, :, :P].reshape(256, 1024)), stream_pairs(up[:, :, P:].reshape(256, 1024))]
    parts += [stream(i["cd_w_out"][0])] + ffn(1)
    for l in (0, 1):
        (fq, fk, fv, ff, fg, dq, dk, dv, dg, mq, mk, mv, mg, gq, gk, gv, ga, gg) = np.split(
            i["w_in_2"][l], np.cumsum([512, 512, 512, 4] + [512] * 9 + [256, 256, 512, 16]), 1)
        parts += [stream(a) for a in (pad(np.concatenate([ga, ga, ff], 1), P), gq, gk, fg, dg, mg, gg)]
        parts += [stream_pairs(a) for a in (fv, dv, mv, gv)]
        parts += [stream(a) for a in (fq, fk, dq, dk, mq, mk, i["w_out_2"][l])]
    return np.concatenate(parts)


def kernel(**inputs):
    import concourse.bacc as bacc
    from concourse.bass_utils import run_bass_kernel_spmd

    i = {name: np.asarray(a) for name, a in inputs.items()}
    arrays = {
        "xT": np.ascontiguousarray(i["x"][0].T.reshape(KT, P, T).transpose(1, 0, 2)),
        "pos": np.ascontiguousarray(np.broadcast_to(i["positions"].astype(np.int32), (P, T))),
        "w": weights(i), "vec": parameters(i), "tab": tables(),
    }
    nc = bacc.Bacc("TRN2", target_bir_lowering=False, num_devices=1)
    args = [nc.dram_tensor(n, a.shape, mybir.dt.from_np(a.dtype), kind="ExternalInput").ap() for n, a in arrays.items()]
    out = nc.dram_tensor("outT", (P, KT, T), mybir.dt.float32, kind="ExternalOutput").ap()
    program(nc, *args, out, arrays["w"].shape[0])
    r = run_bass_kernel_spmd(nc, [arrays], core_ids=[0])
    return r.results[0]["outT"].transpose(1, 0, 2).reshape(D_MODEL, T).T.reshape(1, T, D_MODEL)
```
